# Optimizing a Trainium2 kernel written in Bass

```python
import jax, jax.numpy as jnp
from jax import lax
import numpy as np

D_MODEL = 1024
BATCH = 1
SEQ = 512
DEPTH = 2

N_MIXERS = 2
N_A_LAYERS = (DEPTH + 1) // 2
N_B_LAYERS = DEPTH // 2
RMS_EPS = 1e-6

GLA_HEADS = 4
GLA_DK = D_MODEL // 2 // GLA_HEADS
GLA_DV = D_MODEL // GLA_HEADS
GLA_GATE_RANK = 16
GLA_TAU = 16.0
GLA_CHUNK = 64
GLA_IN = 2 * GLA_HEADS * GLA_DK + 2 * GLA_HEADS * GLA_DV + GLA_GATE_RANK

SWA_HEAD_DIM = 64
SWA_Q_HEADS = D_MODEL // SWA_HEAD_DIM
SWA_KV_HEADS = 2
SWA_GROUP = SWA_Q_HEADS // SWA_KV_HEADS
SWA_WINDOW = 128
SWA_BLOCK = 128
ROPE_THETA = 500000.0
ROPE_DIM = SWA_HEAD_DIM // 4
SWA_IN = (SWA_Q_HEADS + 2 * SWA_KV_HEADS) * SWA_HEAD_DIM

PEER_HEADS = 8
PEER_N_KEYS = 128
PEER_N_EXPERTS = PEER_N_KEYS * PEER_N_KEYS
PEER_QDIM = 128
PEER_HALF = PEER_QDIM // 2
PEER_TOPK = 16
PEER_TOKEN_BLOCK = 128

kernel_name = "hybrid_gla_swa_peer_trunk"

def rms_norm(t, gain):
    t32 = t.astype(jnp.float32)
    y = t32 * lax.rsqrt(jnp.mean(t32 * t32, axis=-1, keepdims=True) + RMS_EPS)
    return (y * gain.astype(jnp.float32)).astype(t.dtype)

def gla_mixer(h, w_in, w_alpha, b_alpha, norm_gain, w_out):
    B, S, _ = h.shape
    H, dk, dv, C = GLA_HEADS, GLA_DK, GLA_DV, GLA_CHUNK
    proj = h @ w_in
    q, k, v, r, lr = jnp.split(proj, [H * dk, 2 * H * dk, 2 * H * dk + H * dv, 2 * H * dk + 2 * H * dv], axis=-1)
    log_a = jax.nn.log_sigmoid((lr @ w_alpha + b_alpha).astype(jnp.float32)) / GLA_TAU
    nc = S // C

    def to_chunks(t, d):
        return t.astype(jnp.float32).reshape(B, nc, C, H, d).transpose(1, 0, 3, 2, 4)

    qc = to_chunks(q, dk) * (dk ** -0.5)
    kc = to_chunks(k, dk)
    vc = to_chunks(v, dv)
    gc = to_chunks(log_a, dk)
    causal = jnp.tril(jnp.ones((C, C), dtype=bool))

    def step(state, xs):
        qb, kb, vb, gb = xs
        b = jnp.cumsum(gb, axis=-2)
        b_last = b[..., -1:, :]
        q_dec = qb * jnp.exp(b)
        k_inv = kb * jnp.exp(-b)
        attn = jnp.where(causal, jnp.einsum('bhid,bhjd->bhij', q_dec, k_inv), 0.0)
        o = jnp.einsum('bhij,bhjv->bhiv', attn, vb) + jnp.einsum('bhid,bhdv->bhiv', q_dec, state)
        k_fwd = kb * jnp.exp(b_last - b)
        state = jnp.exp(b_last[..., 0, :])[..., None] * state + jnp.einsum('bhjd,bhjv->bhdv', k_fwd, vb)
        return state, o

    s0 = jnp.zeros((B, H, dk, dv), jnp.float32)
    _, o = lax.scan(step, s0, (qc, kc, vc, gc))
    o = o.transpose(1, 0, 3, 2, 4).reshape(B, S, H, dv)
    o = rms_norm(o, norm_gain).reshape(B, S, H * dv)
    o = o * jax.nn.silu(r.astype(jnp.float32))
    return o.astype(h.dtype) @ w_out

def apply_partial_rotary(t, cos, sin):
    half = ROPE_DIM // 2
    t32 = t.astype(jnp.float32)
    x1, x2, rest = t32[..., :half], t32[..., half:ROPE_DIM], t32[..., ROPE_DIM:]
    rot = jnp.concatenate([x1 * cos - x2 * sin, x2 * cos + x1 * sin, rest], axis=-1)
    return rot.astype(t.dtype)

def swa_mixer(h, positions, w_in, b_in, q_gain, k_gain, sinks, w_out, b_out):
    B, S, _ = h.shape
    Hq, Hkv, G, hd, BLK = SWA_Q_HEADS, SWA_KV_HEADS, SWA_GROUP, SWA_HEAD_DIM, SWA_BLOCK
    proj = h @ w_in + b_in
    q, k, v = jnp.split(proj, [Hq * hd, (Hq + Hkv) * hd], axis=-1)
    q = rms_norm(q.reshape(B, S, Hq, hd), q_gain)
    k = rms_norm(k.reshape(B, S, Hkv, hd), k_gain)
    v = v.reshape(B, S, Hkv, hd)
    inv_freq = ROPE_THETA ** (-jnp.arange(0, ROPE_DIM, 2, dtype=jnp.float32) / ROPE_DIM)
    ang = positions.astype(jnp.float32)[..., None] * inv_freq
    cos, sin = jnp.cos(ang)[:, :, None, :], jnp.sin(ang)[:, :, None, :]
    q = apply_partial_rotary(q, cos, sin)
    k = apply_partial_rotary(k, cos, sin)

    nb = S // BLK
    qb = q.reshape(B, nb, BLK, Hkv, G, hd)

    def with_prev(t):
        t = t.reshape(B, nb, BLK, Hkv, hd)
        prev = jnp.pad(t[:, :-1], ((0, 0), (1, 0), (0, 0), (0, 0), (0, 0)))
        return jnp.concatenate([prev, t], axis=2)

    kk, vv = with_prev(k), with_prev(v)
    scores = jnp.einsum('bnqhgd,bnkhd->bhgnqk', qb, kk).astype(jnp.float32) * (hd ** -0.5)
    rel = jnp.arange(BLK)[:, None] + BLK - jnp.arange(2 * BLK)[None, :]
    band = (rel >= 0) & (rel < SWA_WINDOW)
    key_pos = jnp.arange(nb)[:, None] * BLK + jnp.arange(2 * BLK)[None, :] - BLK
    mask = band[None] & (key_pos >= 0)[:, None, :]
    scores = jnp.where(mask, scores, -jnp.inf)
    sink = sinks.astype(jnp.float32).reshape(Hkv, G)[None, :, :, None, None]
    m = jnp.maximum(scores.max(axis=-1), sink)
    p = jnp.exp(scores - m[..., None])
    denom = p.sum(axis=-1) + jnp.exp(sink - m)
    p = p / denom[..., None]
    o = jnp.einsum('bhgnqk,bnkhd->bnqhgd', p.astype(vv.dtype), vv).reshape(B, S, Hq * hd)
    return o @ w_out + b_out

def peer_ffn(h, w_q, sub_keys, u, v):
    B, S, D = h.shape
    T = B * S
    K, BLK = PEER_TOPK, PEER_TOKEN_BLOCK
    xt = h.reshape(T // BLK, BLK, D)

    def block(xb):
        q = (xb @ w_q).reshape(BLK, PEER_HEADS, PEER_QDIM)
        s1 = jnp.einsum('thd,hkd->thk', q[..., :PEER_HALF], sub_keys[:, 0]).astype(jnp.float32)
        s2 = jnp.einsum('thd,hkd->thk', q[..., PEER_HALF:], sub_keys[:, 1]).astype(jnp.float32)
        v1, i1 = lax.top_k(s1, K)
        v2, i2 = lax.top_k(s2, K)
        cand = (v1[..., :, None] + v2[..., None, :]).reshape(BLK, PEER_HEADS, K * K)
        sc, ci = lax.top_k(cand, K)
        e = jnp.take_along_axis(i1, ci // K, axis=-1) * PEER_N_KEYS + jnp.take_along_axis(i2, ci % K, axis=-1)
        g = jax.nn.softmax(sc, axis=-1)
        ue = u[e]
        ve = v[e]
        a = jax.nn.gelu(jnp.einsum('thkd,td->thk', ue, xb).astype(jnp.float32), approximate=False) * g
        return jnp.einsum('thk,thkd->td', a.astype(xb.dtype), ve)

    return lax.map(block, xt).reshape(B, S, D)

def setup_inputs(seed: int = 0) -> dict:
    key = jax.random.key(seed)
    ks = jax.random.split(key, 20)
    f32 = jnp.float32
    D = D_MODEL

    def w(k, shape, fan_in):
        return jax.random.normal(k, shape, f32) * (fan_in ** -0.5)

    def gain(k, shape):
        return 1.0 + 0.02 * jax.random.normal(k, shape, f32)

    return {
        "x": jax.random.normal(ks[0], (BATCH, SEQ, D), f32),
        "positions": jnp.broadcast_to(jnp.arange(SEQ, dtype=jnp.int32), (BATCH, SEQ)),
        "ln_mix": gain(ks[1], (DEPTH, D)),
        "ln_ffn": gain(ks[2], (DEPTH, D)),
        "gla_w_in": w(ks[3], (N_A_LAYERS, D, GLA_IN), D),
        "gla_w_alpha": w(ks[4], (N_A_LAYERS, GLA_GATE_RANK, GLA_HEADS * GLA_DK), GLA_GATE_RANK),
        "gla_b_alpha": 0.1 * jax.random.normal(ks[5], (N_A_LAYERS, GLA_HEADS * GLA_DK), f32),
        "gla_norm": gain(ks[6], (N_A_LAYERS, GLA_HEADS, GLA_DV)),
        "gla_w_out": w(ks[7], (N_A_LAYERS, GLA_HEADS * GLA_DV, D), GLA_HEADS * GLA_DV),
        "swa_w_in": w(ks[8], (N_B_LAYERS, D, SWA_IN), D),
        "swa_b_in": 0.02 * jax.random.normal(ks[9], (N_B_LAYERS, SWA_IN), f32),
        "swa_q_norm": gain(ks[10], (N_B_LAYERS, SWA_HEAD_DIM)),
        "swa_k_norm": gain(ks[11], (N_B_LAYERS, SWA_HEAD_DIM)),
        "swa_sinks": 0.5 * jax.random.normal(ks[12], (N_B_LAYERS, SWA_Q_HEADS), f32),
        "swa_w_out": w(ks[13], (N_B_LAYERS, SWA_Q_HEADS * SWA_HEAD_DIM, D), SWA_Q_HEADS * SWA_HEAD_DIM),
        "swa_b_out": 0.02 * jax.random.normal(ks[14], (N_B_LAYERS, D), f32),
        "peer_w_q": w(ks[15], (DEPTH, D, PEER_HEADS * PEER_QDIM), D),
        "peer_keys": w(ks[16], (DEPTH, PEER_HEADS, 2, PEER_N_KEYS, PEER_HALF), PEER_HALF),
        "peer_u": w(ks[17], (DEPTH, PEER_N_EXPERTS, D), D),
        "peer_v": w(ks[18], (DEPTH, PEER_N_EXPERTS, D), D),
    }

def reference(x, positions, ln_mix, ln_ffn, gla_w_in, gla_w_alpha, gla_b_alpha, gla_norm, gla_w_out,
              swa_w_in, swa_b_in, swa_q_norm, swa_k_norm, swa_sinks, swa_w_out, swa_b_out,
              peer_w_q, peer_keys, peer_u, peer_v):
    h = x
    for layer in range(DEPTH):
        j = layer // N_MIXERS
        hn = rms_norm(h, ln_mix[layer])
        if layer % N_MIXERS == 0:
            mix = gla_mixer(hn, gla_w_in[j], gla_w_alpha[j], gla_b_alpha[j], gla_norm[j], gla_w_out[j])
        else:
            mix = swa_mixer(hn, positions, swa_w_in[j], swa_b_in[j], swa_q_norm[j], swa_k_norm[j],
                            swa_sinks[j], swa_w_out[j], swa_b_out[j])
        h = h + mix
        h = h + peer_ffn(rms_norm(h, ln_ffn[layer]), peer_w_q[layer], peer_keys[layer], peer_u[layer], peer_v[layer])
    return h


_drawn_inputs = setup_inputs


def setup_inputs(seed=0):
    import zlib

    import numpy as np

    out = dict(_drawn_inputs(seed))
    spreads = {}
    factors = {'ln_ffn': 8.0,
     'gla_norm': 5.104,
     'swa_b_in': 3.134,
     'swa_q_norm': 8.0,
     'swa_k_norm': 8.0,
     'swa_sinks': 148.375,
     'swa_b_out': 3.37,
     'peer_w_q': 3.1,
     'peer_keys': 3.089,
     'peer_u': 3.403,
     'peer_v': 3.084}
    for name, (base, spread) in spreads.items():
        noise = np.random.default_rng([zlib.crc32(name.encode()), seed]).standard_normal(out[name].shape)
        drawn = base * np.exp(spread * noise) if base else spread * noise
        out[name] = __import__('jax').numpy.asarray(drawn.astype(out[name].dtype))
    for name, factor in factors.items():
        out[name] = (out[name] * factor).astype(out[name].dtype)
    return out
```

```python
from contextlib import ExitStack

import numpy as np

import concourse.bass as bass
from concourse import mybir

F32 = mybir.dt.float32
U32 = mybir.dt.uint32
I32 = mybir.dt.int32
ALU = mybir.AluOpType
ACT = mybir.ActivationFunctionType
AX = mybir.AxisListType.X

P = 128
D = 1024
SEQ = 512
BLOCKS = SEQ // P
KT = D // P
EPS = 1e-6

HEADS_A, DK, DV, CHUNK, RANK, TAU = 4, 128, 256, 64, 16, 16.0
HEADS_Q, HEADS_KV, HD, WINDOW = 16, 2, 64, 128
GROUP = HEADS_Q // HEADS_KV
ROPE_HALF = HD // 4 // 2
THETA = 500000.0

HEADS_P, KEYS, HALF, TOPK = 8, 128, 64, 16
EXPERTS = KEYS * KEYS
PICKS = HEADS_P * TOPK
SLOTS = 8
ROUNDS = PICKS // SLOTS
STAGES = 2 * BLOCKS

STRIP = 256
STRIPS = (20, 13)
RESIDENT = 6
STREAMED = tuple(s - RESIDENT for s in STRIPS)
FREED = ([None, "v", None, None, None, "r", None, None, None, "y", None, "pq0", None, "pq1"],
         [None, None, "y", None, "pq0", None, "pq1"])
HIDDEN = -1e30

SELECT = {
    "pe": ["h2T", "pq0", "pq1", "scores"],
    "act": ["sq2", "sqrt2", "h2T", "pq", "gexp"],
    "dve": ["x2", "var2", "h2", "gshift", "experts"],
}
EVENTS = {
    "gla": {
        "pe": ["hT", "q", "lr", "k", "alpha", "v", "attn", "kfT", "r", "upd", "o", "oT", "y"] + SELECT["pe"],
        "act": ["sq", "sqrt", "hT", "lr", "exp", "ln", "decay", "v", "kf", "silu", "osq", "osqrt", "oT"]
               + SELECT["act"],
        "dve": ["var", "h", "absx", "bdiff", "qd", "kf", "attn", "state0", "state1", "ovar", "o"] + SELECT["dve"],
    },
    "swa": {
        "pe": ["hT", "q", "kv", "qT"] + [f"{w}{g}" for g in range(4) for w in ("s", "pT", "o")]
              + ["oT", "y"] + SELECT["pe"],
        "act": ["sq", "sqrt", "hT", "qsq", "qsqrt", "kprev", "qT"] + [f"{w}{g}" for g in range(4) for w in ("p", "pT")]
               + ["den", "oT"] + SELECT["act"],
        "dve": ["var", "h", "qvar", "v", "qk"] + [f"m{g}" for g in range(4)] + ["o"] + SELECT["dve"],
    },
}


class Prep:

    def __init__(self, kind, p):
        self.kind, self.p = kind, p
        self.layer = 0 if kind == "gla" else 1

    def value(self, engine, event):
        names = EVENTS[self.kind][engine]
        base = 0 if self.kind == "gla" else BLOCKS * len(EVENTS["gla"][engine])
        return self.p * len(names) + (base + names.index(event) + 1)

    def strips_used(self, n):
        per = [f.count(None) for f in FREED]
        before = 0 if self.layer == 0 else BLOCKS * per[0]
        return self.p * per[self.layer] + (before + FREED[self.layer][:n + 1].count(None))

    def slot_uses(self, n):
        slot = n % 2
        per = [(STREAMED[l] + 1 - slot) // 2 for l in (0, 1)]
        return self.p * per[self.layer] + (n // 2 + 1 + (0 if self.layer == 0 else BLOCKS * per[0]))


def alone(eng, passed):
    eng.sem_inc(passed, 1)


class Steps:

    def __init__(self, eng, sem, passed):
        self.eng, self.sem, self.passed, self.n = eng, sem, passed, 0

    def restart(self):
        alone(self.eng, self.passed)
        self.eng.sem_clear(self.sem)
        self.n = 0

    def mark(self, ins):
        self.n += 1
        ins.then_inc(self.sem, 1)

    def settle(self):
        self.eng.wait_ge(self.sem, self.n)

    def __call__(self, ins):
        self.mark(ins)
        self.settle()


def build(nc, x, positions, gain_mix, gain_ffn, strips0, strips1, w_lr, w_alpha, b_alpha, gla_gain,
          b_in, b_out, qk_gain, sinks, keys0, keys1, uv0, uv1, out):
    strips = (strips0, strips1)
    tables = (uv0, uv1)
    h1 = nc.dram_tensor("h1", [SEQ, D], F32, kind="Internal").ap()

    with ExitStack() as ctx:
        def sb(name, shape, dt=F32):
            return ctx.enter_context(nc.sbuf_tensor(name, shape, dt))

        def sem(name):
            return ctx.enter_context(nc.semaphore(name))

        ring = sb("ring", [P, SLOTS, 2 * D])
        pick_now = sb("pick_now", [P, 2, SLOTS], U32)
        pick = sb("pick", [P, BLOCKS * PICKS], U32)
        gate = sb("gate", [P, BLOCKS * PICKS])
        h_now = sb("h_now", [P, D])
        dots = sb("dots", [P, SLOTS])
        gelu = sb("gelu", [P, SLOTS])
        coef = sb("coef", [P, SLOTS])
        diag = sb("diag", [P, 4, P])
        y_sb = sb("y_sb", [P, D])
        resident = sb("resident", [P, RESIDENT, KT, STRIP])
        stream = sb("stream", [P, 2, KT, STRIP])
        arena = sb("arena", [P, 8192])
        xc = sb("xc", [P, D])
        h_next = sb("h_next", [P, D])
        actT = sb("actT", [P, KT, P])
        past = sb("past", [P, 2 * D])
        attnT = sb("attnT", [P, HEADS_A, P])
        keysT = sb("keysT", [P, HEADS_P, KEYS])
        ident = sb("ident", [P, P])
        causal = sb("causal", [P, P])
        band = sb("band", [P, 2 * P])
        ones = sb("ones", [1, P])
        scan_keep = sb("scan_keep", [P, HEADS_A * P])
        iota16 = sb("iota16", [P, TOPK])
        gmix = sb("gmix", [P, 2, KT])
        wlr = sb("wlr", [P, KT, RANK])
        balpha = sb("balpha", [P, HEADS_A])
        ggla = sb("ggla", [P, KT])
        lrT = sb("lrT", [RANK, P])
        gqk = sb("gqk", [P, 2, HD])
        sink = sb("sink", [P, HEADS_Q])
        posi = sb("posi", [P, BLOCKS], I32)
        posf = sb("posf", [P, BLOCKS])
        invf = sb("invf", [P, ROPE_HALF])
        cosb = sb("cosb", [P, BLOCKS * ROPE_HALF])
        sinb = sb("sinb", [P, BLOCKS * ROPE_HALF])
        rope_now = sb("rope_now", [P, 2, ROPE_HALF])
        stat = sb("stat", [P, 6, 24])
        mx = sb("mx", [P, 3, HEADS_Q])

        acc = ctx.enter_context(nc.psum_tensor("acc", [P, D], F32))
        ps = ctx.enter_context(nc.psum_tensor("ps", [P, 6, 512], F32))

        got = [sem(f"got{s}") for s in range(SLOTS)]
        used = [sem(f"used{s}") for s in range(SLOTS)]
        picks_copied = sem("picks_copied")
        started = sem("started")
        dotted = sem("dotted")
        gelued = sem("gelued")
        weighed = sem("weighed")
        diag_ready = sem("diag_ready")
        seeded = sem("seeded")
        acc_taken = sem("acc_taken")
        stored = sem("stored")
        h_taken = sem("h_taken")
        said = {"pe": sem("pe_said"), "act": sem("act_said"), "dve": sem("dve_said")}
        own = {"pe": sem("pe_step"), "act": sem("act_step"), "dve": sem("dve_step"), "pool": sem("pool_step")}
        passed = {e: sem(e + "_passed") for e in own}
        x_loaded = sem("x_loaded")
        gain_loaded = sem("gain_loaded")
        small_loaded = sem("small_loaded")
        bias_loaded = sem("bias_loaded")
        res_loaded = [sem(f"res_loaded{i}") for i in range(RESIDENT)]
        slot_loaded = [sem(f"slot_loaded{i}") for i in range(2)]
        strip_used = sem("strip_used")
        consts_loaded = sem("consts_loaded")
        keys_loaded = sem("keys_loaded")
        consts_made = sem("consts_made")
        consts_act = sem("consts_act")
        consts_dve = sem("consts_dve")
        band_made = sem("band_made")

        N_CONST_LOADS = 7
        N_CONST_MADE = 15

        def area(lo, *dims):
            n = int(np.prod(dims))
            v = arena[:, lo:lo + n]
            if len(dims) == 2:
                return v.rearrange("p (a b) -> p a b", a=dims[0])
            if len(dims) == 3:
                return v.rearrange("p (a b c) -> p a b c", a=dims[0], b=dims[1])
            return v

        g_v = area(0, HEADS_A, DV)
        g_r = area(1024, HEADS_A, DV)
        g_o = area(2048, HEADS_A, DV)
        hn = area(3072, KT, P)
        angle = area(7680, 4, BLOCKS, ROPE_HALF)
        g_b = area(4096, HEADS_A, P)
        g_t = area(4608, HEADS_A, P)
        g_eb = area(5120, HEADS_A, P)
        g_enb = area(5632, HEADS_A, P)
        g_ef = area(6144, HEADS_A, P)
        g_qd = area(6656, HEADS_A, P)
        g_kinv = area(7168, HEADS_A, P)
        g_kf = area(7680, HEADS_A, P)
        walpha = arena[0:RANK, 6656:7168]
        g_kft = area(4096, HEADS_A, DK)
        junk = area(2048, D)
        ffn_gain = area(5120, D)
        s_qk = area(0, HEADS_Q + HEADS_KV, HD)
        s_sq = area(1152, HEADS_Q + HEADS_KV, HD)
        s_qT = area(1152, KT, P)
        s_p = [area(2304 + 1024 * i, 4, 2 * P) for i in range(2)]
        s_kdup = area(4352, HEADS_KV, 2, HD)
        s_pT = [area(4352 + 1024 * i, 8, P) for i in range(2)]
        s_o = area(6400, HEADS_Q, HD)
        bias_in = arena[0:1, 4352:5632]
        bias_out = arena[0:1, 4096:5120]
        s_rope = area(7424, 4, HEADS_Q + HEADS_KV, ROPE_HALF)
        pqT = area(0, HEADS_P, P)
        c_rest = area(1024, KT, KEYS)
        cand = area(2048, HEADS_P, TOPK, TOPK)
        cand_rest = area(4096, HEADS_P, TOPK * TOPK)
        onehot = area(6144, HEADS_P * TOPK, TOPK)
        top = area(0, 2 * HEADS_P, TOPK)
        topi = area(256, 2 * HEADS_P, TOPK).bitcast(U32)
        topf = area(512, 2 * HEADS_P, TOPK)
        best = area(768, HEADS_P, TOPK)
        besti = area(896, HEADS_P, TOPK).bitcast(U32)
        ab = area(1024, 2, HEADS_P, TOPK).bitcast(U32)
        abf = area(1280, 2, HEADS_P, TOPK)
        ef = area(1536, 2, HEADS_P, TOPK)
        gsm = area(1792, 2, HEADS_P)

        state0 = past[:, 0:D].rearrange("p (h v) -> p h v", h=HEADS_A)
        state1 = past[:, D:2 * D].rearrange("p (h v) -> p h v", h=HEADS_A)
        kT = past[:, 0:2 * 2 * P].rearrange("p (h t) -> p h t", h=HEADS_KV)
        vv = past[:, D:D + 2 * P].rearrange("p (b n) -> p b n", b=2)

        def two_banks(a, b):
            return ps[:, a:b + 1, :].rearrange("p a n -> p (a n)")

        def said_by(eng, who, prep, event):
            eng.wait_ge(said[who], prep.value(who, event))

        def before(prep):
            if isinstance(prep.p, int) and prep.layer == 1:
                return Prep("gla", BLOCKS - 1)
            return Prep(prep.kind, prep.p - 1)

        def weight(prep, n):
            if n < RESIDENT:
                return resident[:, n]
            return stream[:, (n - RESIDENT) % 2]

        def out0(prep):
            return 12 if prep.layer == 0 else 5

        def pq0(prep):
            return 16 if prep.layer == 0 else 9

        block = ctx.enter_context(nc.Block())

        @block.sync
        def _(sp):
            for dst, src in ((gmix[:], gain_mix), (wlr[:], w_lr), (balpha[:], b_alpha),
                             (ggla[:], gla_gain),
                             (gqk[:].rearrange("p a d -> p (a d)"), qk_gain.to_broadcast([P, 2 * HD])),
                             (sink[:], sinks.to_broadcast([P, HEADS_Q])), (posi[:], positions)):
                sp.dma_start(dst, src).then_inc(consts_loaded, 16)
            sp.dma_start(keysT[:], keys0).then_inc(keys_loaded, 16)

            def freed(prep, n):
                event = FREED[prep.layer][n]
                if event is None:
                    sp.wait_ge(strip_used, prep.strips_used(n))
                else:
                    said_by(sp, "pe", prep, event)

            def preps(prep):
                first = isinstance(prep.p, int)
                src = x if prep.layer == 0 else h1
                stage = prep.p + BLOCKS * prep.layer
                if not (first and prep.layer == 0):
                    sp.wait_ge(seeded, stage)
                if prep.layer == 1:
                    sp.wait_ge(stored, prep.p * 16 + 16)
                sp.dma_start(xc[:], src[bass.ds(prep.p * P, P), :]).then_inc(x_loaded, 16)
                if not (first and prep.layer == 0):
                    said_by(sp, "dve", before(prep), "experts")
                if prep.layer == 0:
                    sp.dma_start(walpha, w_alpha).then_inc(small_loaded, 16)
                else:
                    sp.dma_start(bias_in, b_in).then_inc(small_loaded, 16)
                if first and prep.layer == 1:
                    said_by(sp, "pe", Prep("gla", BLOCKS - 1), "scores")
                    sp.dma_start(keysT[:], keys1).then_inc(keys_loaded, 16)
                if first:
                    for n in range(RESIDENT):
                        sp.dma_start(resident[:, n].rearrange("p k c -> p (k c)"), strips[prep.layer][n])\
                          .then_inc(res_loaded[n], 16)
                for n in range(STREAMED[prep.layer]):
                    if n == STREAMED[prep.layer] - 5:
                        said_by(sp, "pe", prep, "oT")
                        sp.dma_start(ffn_gain, gain_ffn[prep.layer:prep.layer + 1, :].to_broadcast([P, D]))\
                          .then_inc(gain_loaded, 16)
                        if prep.layer == 1:
                            sp.dma_start(bias_out, b_out).then_inc(bias_loaded, 16)
                    if n >= 2:
                        freed(prep, n - 2)
                    elif not (first and prep.layer == 0):
                        last = STREAMED[before(prep).layer] - 1
                        freed(before(prep), last if last % 2 == n else last - 1)
                    sp.dma_start(stream[:, n % 2].rearrange("p k c -> p (k c)"),
                                 strips[prep.layer][RESIDENT + n]).then_inc(slot_loaded[n % 2], 16)

            def close(s, layer):
                sp.wait_ge(acc_taken, s * 2 + 2)
                dst = h1 if layer == 0 else out
                sp.dma_start(dst[bass.ds((s - layer * BLOCKS) * P, P), :], y_sb[:]).then_inc(stored, 16)

            preps(Prep("gla", 0))
            with sp.Fori(0, BLOCKS - 1) as s:
                preps(Prep("gla", s + 1))
                close(s, 0)
            preps(Prep("swa", 0))
            close(BLOCKS - 1, 0)
            with sp.Fori(BLOCKS, STAGES - 1) as s:
                preps(Prep("swa", s - (BLOCKS - 1)))
                close(s, 1)
            close(STAGES - 1, 1)
            sp.wait_ge(stored, 16 * STAGES)

        @block.gpsimd
        def _(pool):
            step = Steps(pool, own["pool"], passed["pool"])
            made = [0]

            def const(ins):
                made[0] += 1
                ins.then_inc(consts_made, 1)
                pool.wait_ge(consts_made, made[0])

            const(pool.memset(ident[:], 0.0))
            const(pool.affine_select(out=ident[:], in_=ident[:], compare_op=ALU.not_equal, fill=1.0, base=0,
                                     pattern=[[-1, P]], channel_multiplier=1))
            const(pool.memset(causal[:], 1.0))
            const(pool.affine_select(out=causal[:], in_=causal[:], compare_op=ALU.is_ge, fill=0.0, base=0,
                                     pattern=[[1, P]], channel_multiplier=-1))
            const(pool.memset(causal[0:CHUNK, CHUNK:P], 0.0))
            const(pool.memset(band[:, 0:P], HIDDEN))
            const(pool.memset(band[:, P:2 * P], 0.0))
            const(pool.affine_select(out=band[:, P:2 * P], in_=band[:, P:2 * P], compare_op=ALU.is_ge, fill=HIDDEN,
                                     base=0, pattern=[[-1, P]], channel_multiplier=1))
            const(pool.memset(ones[:], 1.0))
            const(pool.memset(scan_keep[:], 1.0))
            const(pool.memset(scan_keep[:].rearrange("p (c t) -> p c t", t=CHUNK)[:, :, 0:1], 0.0))
            const(pool.iota(iota16[:], [[1, TOPK]], base=0, channel_multiplier=0,
                            allow_small_or_imprecise_dtypes=True))
            const(pool.memset(attnT[:], 0.0))
            const(pool.memset(past[:], 0.0))
            for j in range(ROPE_HALF):
                f = float(np.float32(THETA) ** np.float32(-2.0 * j / (2 * ROPE_HALF)))
                last = pool.memset(invf[:, j:j + 1], f)
                if j < ROPE_HALF - 1:
                    step(last)
            const(last)
            assert made[0] == N_CONST_MADE
            for i in range(SLOTS):
                pool.memset(pick_now[:, 0, i:i + 1], 0).then_inc(used[i], 1)
            pool.memset(pick_now[:, 1, :], 0).then_inc(started, 1)

            def stage(s, prep, layer):
                said_by(pool, "dve", prep, "experts")
                alone(pool, passed["pool"])
                base = s * (ROUNDS // 2)
                with pool.Fori(0, ROUNDS // 2) as pair:
                    for half in range(2):
                        n = (base + pair) * 2 + half
                        step.restart()
                        step(pool.tensor_copy(
                            pick_now[:, half, :],
                            pick[:, bass.ds((base + pair) * (2 * SLOTS) + (half * SLOTS - layer * BLOCKS * PICKS),
                                            SLOTS)]))
                        for i in range(SLOTS):
                            pool.wait_ge(used[i], n + 1)
                            alone(pool, passed["pool"])
                            pool.indirect_dma_start(
                                ring[:, i, :], None, tables[layer],
                                bass.IndirectOffsetOnAxis(ap=pick_now[:, half, i:i + 1], axis=0),
                            ).then_inc(got[i], 16)

            pool.wait_ge(started, 1)
            with pool.Fori(0, BLOCKS) as s:
                stage(s, Prep("gla", s), 0)
            said_by(pool, "dve", Prep("swa", 0), "experts")
            step.restart()
            step(pool.memset(band[:, 0:P], 0.0))
            pool.affine_select(out=band[:, 0:P], in_=band[:, 0:P], compare_op=ALU.is_ge, fill=HIDDEN, base=-1,
                               pattern=[[1, P]], channel_multiplier=-1).then_inc(band_made, 1)
            with pool.Fori(BLOCKS, STAGES) as s:
                stage(s, Prep("swa", s - BLOCKS), 1)

        @block.vector
        def _(dve):
            step = Steps(dve, own["dve"], passed["dve"])

            def say(prep, event, ins):
                ins.then_inc(said["dve"], 1)

            def root(prep, n, scale, var_event, sqrt_event):
                v, r, t, u = stat[:, 1, 0:n], stat[:, 3, 0:n], stat[:, 4, 0:n], stat[:, 5, 0:n]
                say(prep, var_event, dve.tensor_scalar(v, stat[:, 0, 0:n], scale, EPS, ALU.mult, ALU.add))
                said_by(dve, "dve", prep, var_event)
                said_by(dve, "act", prep, sqrt_event)
                step(dve.reciprocal(r, stat[:, 2, 0:n]))
                step(dve.tensor_tensor(t, r, r, ALU.mult))
                step(dve.tensor_tensor(u, t, v, ALU.mult))
                step(dve.tensor_scalar(t, u, -0.5, 1.5, ALU.mult, ALU.add))
                step(dve.tensor_tensor(v, r, t, ALU.mult))
                return v

            def normed(prep):
                said_by(dve, "act", prep, "sq")
                r = root(prep, 1, 1.0 / D, "var", "sqrt")
                say(prep, "h", dve.tensor_scalar(hn.rearrange("p k t -> p (k t)"), xc[:], r, None, ALU.mult))

            def gla(prep):
                step.restart()
                normed(prep)
                yield 1
                yield 1
                said_by(dve, "pe", prep, "alpha")
                for h in range(HEADS_A):
                    step.mark(dve.tensor_scalar(g_b[:, h], ps[:, 5, h * P:(h + 1) * P], balpha[:, h:h + 1], None,
                                                ALU.add))
                step.settle()
                say(prep, "absx", dve.scalar_tensor_tensor(g_t, g_b, -1.0, g_b, ALU.mult, ALU.max))
                said_by(dve, "act", prep, "ln")
                step(dve.scalar_tensor_tensor(g_b, g_b, 0.0, g_t, ALU.min, ALU.subtract))
                step(dve.tensor_tensor_scan(g_t.rearrange("p h t -> p (h t)"), scan_keep[:],
                                            g_b.rearrange("p h t -> p (h t)"), 0.0, ALU.mult, ALU.add))
                chunks = g_t.rearrange("p h (c t) -> p (h c) t", c=P // CHUNK)
                say(prep, "bdiff", dve.tensor_tensor(
                    g_b.rearrange("p h (c t) -> p (h c) t", c=P // CHUNK),
                    chunks[:, :, CHUNK - 1:CHUNK].to_broadcast([P, HEADS_A * P // CHUNK, CHUNK]), chunks,
                    ALU.subtract))
                yield 1
                said_by(dve, "act", prep, "decay")
                q, k = ps[:, 2, :].rearrange("p (h t) -> p h t", h=HEADS_A), \
                    ps[:, 3, :].rearrange("p (h t) -> p h t", h=HEADS_A)
                step.mark(dve.scalar_tensor_tensor(g_qd, q, DK ** -0.5, g_eb, ALU.mult, ALU.mult))
                say(prep, "qd", dve.tensor_tensor(g_kinv, k, g_enb, ALU.mult))
                said_by(dve, "dve", prep, "qd")
                step.settle()
                say(prep, "kf", dve.tensor_tensor(g_kf, k, g_ef, ALU.mult))
                said_by(dve, "pe", prep, "attn")
                alone(dve, passed["dve"])
                say(prep, "attn", dve.copy_predicated(
                    attnT[:], causal[:].bitcast(U32).rearrange("p (o t) -> p o t", o=1).to_broadcast([P, HEADS_A, P]),
                    ps[:, 4, :].rearrange("p (h t) -> p h t", h=HEADS_A)))
                yield 1
                said_by(dve, "pe", prep, "upd")
                last = g_eb.rearrange("p h (c t) -> p h c t", c=2)
                for h in range(HEADS_A):
                    i = dve.scalar_tensor_tensor(state1[:, h], state0[:, h], last[:, h, 0, CHUNK - 1:CHUNK],
                                                 two_banks(0, 1)[:, h * DV:(h + 1) * DV], ALU.mult, ALU.add)
                    if h < HEADS_A - 1:
                        step.mark(i)
                say(prep, "state0", i)
                said_by(dve, "dve", prep, "state0")
                step.settle()
                yield 1
                said_by(dve, "pe", prep, "o")
                for h in range(HEADS_A):
                    i = dve.scalar_tensor_tensor(state0[:, h], state1[:, h], last[:, h, 1, CHUNK - 1:CHUNK],
                                                 two_banks(4, 5)[:, h * DV:(h + 1) * DV], ALU.mult, ALU.add)
                    if h < HEADS_A - 1:
                        step.mark(i)
                say(prep, "state1", i)
                said_by(dve, "dve", prep, "state1")
                step.settle()
                said_by(dve, "act", prep, "osq")
                r = root(prep, HEADS_A, 1.0 / DV, "ovar", "osqrt")
                for h in range(HEADS_A):
                    i = dve.scalar_tensor_tensor(g_o[:, h], two_banks(2, 3)[:, h * DV:(h + 1) * DV], r[:, h:h + 1],
                                                 g_r[:, h], ALU.mult, ALU.mult)
                    if h < HEADS_A - 1:
                        step.mark(i)
                say(prep, "o", i)
                said_by(dve, "dve", prep, "o")
                step.settle()
                yield 1
                yield from select(prep)

            def swa(prep):
                step.restart()
                normed(prep)
                step(dve.tensor_copy(rope_now[:, 0, :], cosb[:, bass.ds(prep.p * ROPE_HALF, ROPE_HALF)]))
                step(dve.tensor_copy(rope_now[:, 1, :], sinb[:, bass.ds(prep.p * ROPE_HALF, ROPE_HALF)]))
                yield 1
                yield 1
                NH = HEADS_Q + HEADS_KV
                said_by(dve, "act", prep, "qsq")
                step(dve.tensor_reduce(stat[:, 0, 0:NH], s_sq, AX, ALU.add))
                r = root(prep, NH, 1.0 / HD, "qvar", "qsqrt")
                rb = r.rearrange("p (h o) -> p h o", o=1)
                q = two_banks(0, 1).rearrange("p (h d) -> p h d", h=HEADS_Q)
                k = ps[:, 2, 0:HEADS_KV * HD].rearrange("p (h d) -> p h d", h=HEADS_KV)
                step.mark(dve.tensor_tensor(s_qk[:, 0:HEADS_Q], q, rb[:, 0:HEADS_Q].to_broadcast([P, HEADS_Q, HD]),
                                            ALU.mult))
                step.mark(dve.tensor_tensor(s_qk[:, HEADS_Q:NH], k,
                                            rb[:, HEADS_Q:NH].to_broadcast([P, HEADS_KV, HD]), ALU.mult))
                step(dve.tensor_copy(vv[:, 0, :], vv[:, 1, :]))
                say(prep, "v", dve.tensor_copy(vv[:, 1, :], ps[:, 2, HEADS_KV * HD:2 * HEADS_KV * HD]))
                step.mark(dve.tensor_tensor(s_qk[:, 0:HEADS_Q], s_qk[:, 0:HEADS_Q],
                                            gqk[:, 0:1, :].to_broadcast([P, HEADS_Q, HD]), ALU.mult))
                step.mark(dve.tensor_tensor(s_qk[:, HEADS_Q:NH], s_qk[:, HEADS_Q:NH],
                                            gqk[:, 1:2, :].to_broadcast([P, HEADS_KV, HD]), ALU.mult))
                step.settle()
                x1, x2 = s_qk[:, :, 0:ROPE_HALF], s_qk[:, :, ROPE_HALF:2 * ROPE_HALF]
                cb = rope_now[:, 0:1, :].to_broadcast([P, NH, ROPE_HALF])
                sb_ = rope_now[:, 1:2, :].to_broadcast([P, NH, ROPE_HALF])
                for i, (a, b) in enumerate(((x1, cb), (x2, sb_), (x2, cb), (x1, sb_))):
                    step.mark(dve.tensor_tensor(s_rope[:, i], a, b, ALU.mult))
                step.settle()
                step.mark(dve.tensor_tensor(x1, s_rope[:, 0], s_rope[:, 1], ALU.subtract))
                step.mark(dve.tensor_tensor(x2, s_rope[:, 2], s_rope[:, 3], ALU.add))
                step.settle()
                kk = s_qk[:, HEADS_Q:NH]
                step(dve.tensor_copy(s_kdup[:, :, 0, :], kk))
                say(prep, "qk", dve.tensor_copy(s_kdup[:, :, 1, :], kk))
                yield 1
                yield 1
                for g in range(4):
                    if g == 2:
                        yield 1
                    if g >= 2:
                        said_by(dve, "pe", prep, f"pT{g - 2}")
                    said_by(dve, "pe", prep, f"s{g}")
                    sc = ps[:, 0:2, :].rearrange("p b (h t) -> p (b h) t", h=2)
                    step(dve.scalar_tensor_tensor(
                        s_p[g % 2], sc, HD ** -0.5,
                        band[:].rearrange("p (o t) -> p o t", o=1).to_broadcast([P, 4, 2 * P]), ALU.mult, ALU.add))
                    m = mx[:, 0, 4 * g:4 * g + 4]
                    step(dve.tensor_reduce(m, s_p[g % 2], AX, ALU.max))
                    for par in range(2):
                        step.mark(dve.tensor_tensor(m[:, 2 * par:2 * par + 2], m[:, 2 * par:2 * par + 2],
                                                    sink[:, 4 * g + par:4 * g + 4:2], ALU.max))
                    step.settle()
                    for par in range(2):
                        step.mark(dve.tensor_tensor(mx[:, 1, 4 * g + 2 * par:4 * g + 2 * par + 2],
                                                    sink[:, 4 * g + par:4 * g + 4:2], m[:, 2 * par:2 * par + 2],
                                                    ALU.subtract))
                    step.settle()
                    say(prep, f"m{g}", dve.tensor_scalar(m, m, -1.0, None, ALU.mult))
                said_by(dve, "act", prep, "den")
                step(dve.tensor_tensor(stat[:, 4, 0:HEADS_Q], mx[:, 1, :], mx[:, 2, :], ALU.add))
                step(dve.reciprocal(stat[:, 5, 0:HEADS_Q], stat[:, 4, 0:HEADS_Q]))
                said_by(dve, "pe", prep, "o3")
                rd = stat[:, 5, 0:HEADS_Q].rearrange("p (g a b o) -> p g a b o", g=4, a=2, o=1)
                oo = s_o.rearrange("p (g b a) d -> p g b a d", g=4, a=2)
                pp = two_banks(4, 5).rearrange("p (g b a d) -> p g b a d", g=4, b=2, a=2)
                for g in range(4):
                    for par in range(2):
                        i = dve.tensor_tensor(oo[:, g, :, par, :], pp[:, g, :, par, :],
                                              rd[:, g, par].to_broadcast([P, 2, HD]), ALU.mult)
                        if (g, par) != (3, 1):
                            step.mark(i)
                step.settle()
                say(prep, "o", i)
                said_by(dve, "dve", prep, "o")
                yield 1
                yield from select(prep)

            def select(prep):
                yield 1
                said_by(dve, "pe", prep, "y")
                for b in range(2):
                    i = dve.tensor_tensor(xc[:, b * 512:(b + 1) * 512], xc[:, b * 512:(b + 1) * 512],
                                          ps[:, 4 + b, :], ALU.add)
                    if b == 0:
                        step.mark(i)
                say(prep, "x2", i)
                said_by(dve, "dve", prep, "x2")
                step.settle()
                said_by(dve, "act", prep, "sq2")
                r = root(prep, 1, 1.0 / D, "var2", "sqrt2")
                dve.wait_ge(gain_loaded, (prep.p + prep.layer * BLOCKS) * 16 + 16)
                say(prep, "h2", dve.scalar_tensor_tensor(h_next[:], xc[:], r, ffn_gain, ALU.mult, ALU.mult))
                said_by(dve, "dve", prep, "h2")
                yield 1
                yield 1

                def score(v):
                    half, h = v // HEADS_P, v % HEADS_P
                    return ps[:, 4 * half + h // 4, (h % 4) * KEYS:(h % 4 + 1) * KEYS]

                said_by(dve, "pe", prep, "scores")
                alone(dve, passed["dve"])
                for part in range(2):
                    vs = range(part * 8, part * 8 + 8)
                    for v in vs:
                        step.mark(dve.max(top[:, v, 0:8], score(v)))
                    step.settle()
                    for v in vs:
                        step.mark(dve.max_index(topi[:, v, 0:8], top[:, v, 0:8], score(v)))
                        step.mark(dve.match_replace(c_rest[:, v % 8], top[:, v, 0:8], score(v), -3.0e38))
                    step.settle()
                    for v in vs:
                        step.mark(dve.max(top[:, v, 8:16], c_rest[:, v % 8]))
                    step.settle()
                    for v in vs:
                        step.mark(dve.max_index(topi[:, v, 8:16], top[:, v, 8:16], c_rest[:, v % 8]))
                    step.settle()
                    yield 1
                step.mark(dve.tensor_copy(topf[:], topi[:]))
                for h in range(HEADS_P):
                    step.mark(dve.tensor_tensor(
                        cand[:, h], top[:, h, :].rearrange("p (a o) -> p a o", o=1).to_broadcast([P, TOPK, TOPK]),
                        top[:, HEADS_P + h, :].rearrange("p (o b) -> p o b", o=1).to_broadcast([P, TOPK, TOPK]),
                        ALU.add))
                step.settle()
                for part in range(2):
                    hs = range(part * 4, part * 4 + 4)
                    flat = cand.rearrange("p h a b -> p h (a b)")
                    for h in hs:
                        step.mark(dve.max(best[:, h, 0:8], flat[:, h]))
                    step.settle()
                    for h in hs:
                        step.mark(dve.max_index(besti[:, h, 0:8], best[:, h, 0:8], flat[:, h]))
                        step.mark(dve.match_replace(cand_rest[:, h], best[:, h, 0:8], flat[:, h], -3.0e38))
                    step.settle()
                    for h in hs:
                        step.mark(dve.max(best[:, h, 8:16], cand_rest[:, h]))
                    step.settle()
                    for h in hs:
                        step.mark(dve.max_index(besti[:, h, 8:16], best[:, h, 8:16], cand_rest[:, h]))
                    step.settle()
                    if part == 0:
                        yield 1
                say(prep, "gshift", dve.tensor_tensor(ef[:, 0], best[:], best[:, :, 0:1].to_broadcast(
                    [P, HEADS_P, TOPK]), ALU.subtract))
                step.mark(dve.tensor_scalar(ab[:, 0], besti[:], 4, None, ALU.logical_shift_right))
                step.mark(dve.tensor_scalar(ab[:, 1], besti[:], TOPK - 1, None, ALU.bitwise_and))
                step.settle()
                step(dve.tensor_copy(abf[:], ab[:]))
                said_by(dve, "act", prep, "gexp")
                step(dve.tensor_reduce(gsm[:, 0], ef[:, 1], AX, ALU.add))
                step(dve.reciprocal(gsm[:, 1], gsm[:, 0]))
                step(dve.tensor_tensor(
                    gate[:, bass.ds(prep.p * PICKS, PICKS)].rearrange("p (h k) -> p h k", h=HEADS_P), ef[:, 1],
                    gsm[:, 1, :].rearrange("p (h o) -> p h o", o=1).to_broadcast([P, HEADS_P, TOPK]), ALU.mult))
                yield 2
                for half in range(2):
                    for h in range(HEADS_P):
                        step.mark(dve.tensor_tensor(
                            onehot[:, h * TOPK:(h + 1) * TOPK, :],
                            abf[:, half, h, :].rearrange("p (k o) -> p k o", o=1).to_broadcast([P, TOPK, TOPK]),
                            iota16[:].rearrange("p (o j) -> p o j", o=1).to_broadcast([P, TOPK, TOPK]),
                            ALU.is_equal))
                    step.settle()
                    for h in range(HEADS_P):
                        o = onehot[:, h * TOPK:(h + 1) * TOPK, :]
                        step.mark(dve.tensor_tensor(
                            o, o, topf[:, half * HEADS_P + h, :].rearrange("p (o j) -> p o j", o=1).to_broadcast(
                                [P, TOPK, TOPK]), ALU.mult))
                    step.settle()
                    step(dve.tensor_reduce(ef[:, half].rearrange("p h k -> p (h k)"), onehot, AX, ALU.add))
                step(dve.scalar_tensor_tensor(ef[:, 0], ef[:, 0], float(KEYS), ef[:, 1], ALU.mult, ALU.add))
                say(prep, "experts", dve.tensor_copy(pick[:, bass.ds(prep.p * PICKS, PICKS)],
                                                     ef[:, 0].rearrange("p h k -> p (h k)")))

            def preps(prep):
                return gla(prep) if prep.kind == "gla" else swa(prep)

            def take_h(s):
                if not (isinstance(s, int) and s == 0):
                    dve.wait_ge(dotted, s * PICKS)
                dve.tensor_copy(h_now[:], h_next[:]).then_inc(h_taken, 1)
                dve.wait_ge(h_taken, s + 1)

            def rounds(s, lo, n):
                def one(r):
                    for i in range(SLOTS):
                        dve.wait_ge(got[i], (s * ROUNDS + r) * 16 + 16)
                        dve.tensor_tensor_reduce(ring[:, i, 0:D], ring[:, i, 0:D], h_now[:], 1.0, 0.0, ALU.mult,
                                                 ALU.add, dots[:, i:i + 1]).then_inc(dotted, 1)
                if n == 1:
                    one(lo)
                else:
                    with dve.Fori(lo, lo + n) as r:
                        one(r)

            dve.wait_ge(consts_made, N_CONST_MADE)
            dve.wait_ge(consts_loaded, 16 * N_CONST_LOADS)
            step.restart()
            step(dve.tensor_copy(posf[:], posi[:]))
            for b in range(BLOCKS):
                step.mark(dve.tensor_scalar(angle[:, 0, b, :], invf[:], posf[:, b:b + 1], None, ALU.mult))
            step.settle()
            TWO_PI = 2.0 * np.pi
            c1 = 6.28125
            c2 = float(np.float32(TWO_PI - c1) - np.float32(TWO_PI - c1) % np.float32(2.0 ** -20))
            c3 = float(TWO_PI - c1 - c2)
            ROUND = 1.5 * 2.0 ** 23
            PI = 3.1415925
            for w, turn in ((1, 0.0), (2, 0.25)):
                a, k = angle[:, w], angle[:, 3]
                step(dve.tensor_scalar(k, angle[:, 0], 1.0 / TWO_PI, turn, ALU.mult, ALU.add))
                step(dve.tensor_scalar(k, k, ROUND, None, ALU.add))
                step(dve.tensor_scalar(k, k, ROUND, None, ALU.subtract))
                step(dve.scalar_tensor_tensor(a, k, -c1, angle[:, 0], ALU.mult, ALU.add))
                step(dve.scalar_tensor_tensor(a, k, -c2, a, ALU.mult, ALU.add))
                step(dve.scalar_tensor_tensor(a, k, -c3, a, ALU.mult, ALU.add))
                step(dve.tensor_scalar(a, a, turn * TWO_PI, PI, ALU.add, ALU.min))
                step(dve.tensor_scalar(a, a, -PI, None, ALU.max))
            dve.memset(dots[:], 0.0).then_inc(consts_dve, 1)
            dve.wait_ge(consts_dve, 1)
            dve.wait_ge(consts_act, 2)

            def stage(s, prep):
                take_h(s)
                lo = 0
                if prep is not None:
                    for n in preps(prep):
                        rounds(s, lo, n)
                        lo += n
                if lo < ROUNDS:
                    rounds(s, lo, ROUNDS - lo)

            for _ in preps(Prep("gla", 0)):
                pass
            with dve.Fori(0, BLOCKS - 1) as s:
                stage(s, Prep("gla", s + 1))
            stage(BLOCKS - 1, Prep("swa", 0))
            with dve.Fori(BLOCKS, STAGES - 1) as s:
                dve.wait_ge(band_made, 1)
                stage(s, Prep("swa", s - (BLOCKS - 1)))
            stage(STAGES - 1, None)

        @block.scalar
        def _(act):
            step = Steps(act, own["act"], passed["act"])

            def say(ins):
                ins.then_inc(said["act"], 1)

            def sqrt(prep, n, var_event):
                said_by(act, "dve", prep, var_event)
                say(act.activation(stat[:, 2, 0:n], stat[:, 1, 0:n], ACT.Sqrt))

            def turned(prep, event, gain=None, at=0):
                said_by(act, "pe", prep, event)
                for k in range(KT):
                    src = ps[:, at + k // 4, (k % 4) * P:(k % 4 + 1) * P]
                    scale = 1.0 if gain is None else gain[:, k:k + 1]
                    i = act.activation(actT[:, k, :], src, ACT.Copy, scale=scale)
                    if k < KT - 1:
                        step.mark(i)
                step.settle()
                say(i)

            def normed(prep):
                act.wait_ge(x_loaded, (prep.p + prep.layer * BLOCKS) * 16 + 16)
                say(act.activation(junk, xc[:], ACT.Square, accum_out=stat[:, 0, 0:1]))
                sqrt(prep, 1, "var")
                turned(prep, "hT", gmix[:, prep.layer])

            def gla(prep):
                step.restart()
                normed(prep)
                yield 1
                said_by(act, "pe", prep, "lr")
                say(act.activation(lrT[:], ps[0:RANK, 4, 0:P], ACT.Copy))
                yield 1
                said_by(act, "dve", prep, "absx")
                say(act.activation(g_t, g_t, ACT.Exp, scale=-1.0))
                said_by(act, "act", prep, "exp")
                say(act.activation(g_t, g_t, ACT.Ln, bias=1.0))
                said_by(act, "dve", prep, "bdiff")
                step.mark(act.activation(g_eb, g_t, ACT.Exp, scale=1.0 / TAU))
                step.mark(act.activation(g_enb, g_t, ACT.Exp, scale=-1.0 / TAU))
                step.settle()
                say(act.activation(g_ef, g_b, ACT.Exp, scale=1.0 / TAU))
                said_by(act, "pe", prep, "v")
                say(act.activation(g_v.rearrange("p h v -> p (h v)"), two_banks(0, 1), ACT.Copy))
                yield 1
                said_by(act, "pe", prep, "kfT")
                say(act.activation(g_kft, ps[:, 5, :].rearrange("p (h t) -> p h t", h=HEADS_A), ACT.Copy))
                yield 1
                said_by(act, "pe", prep, "r")
                say(act.activation(g_r.rearrange("p h v -> p (h v)"), two_banks(2, 3), ACT.Silu))
                yield 1
                said_by(act, "pe", prep, "o")
                for h in range(HEADS_A):
                    i = act.activation(hn.rearrange("p k t -> p (k t)")[:, h * DV:(h + 1) * DV],
                                       two_banks(2, 3)[:, h * DV:(h + 1) * DV], ACT.Square,
                                       accum_out=stat[:, 0, h:h + 1])
                    if h < HEADS_A - 1:
                        step.mark(i)
                step.settle()
                say(i)
                sqrt(prep, HEADS_A, "ovar")
                turned(prep, "oT", ggla)
                yield 1
                yield from select(prep)

            def swa(prep):
                step.restart()
                normed(prep)
                yield 1
                yield 1
                said_by(act, "pe", prep, "q")
                step.mark(act.activation(s_sq[:, 0:HEADS_Q].rearrange("p h d -> p (h d)"), two_banks(0, 1),
                                         ACT.Square))
                said_by(act, "pe", prep, "kv")
                i = act.activation(s_sq[:, HEADS_Q:].rearrange("p h d -> p (h d)"), ps[:, 2, 0:HEADS_KV * HD],
                                   ACT.Square)
                step.settle()
                say(i)
                sqrt(prep, HEADS_Q + HEADS_KV, "qvar")
                say(act.activation(kT[:, :, 0:P], kT[:, :, P:2 * P], ACT.Copy))
                yield 1
                said_by(act, "pe", prep, "qT")
                said_by(act, "act", prep, "kprev")
                step(act.activation(kT[:, :, P:2 * P], ps[:, 2, 0:HEADS_KV * P].rearrange(
                    "p (h t) -> p h t", h=HEADS_KV), ACT.Copy))
                say(act.activation(s_qT.rearrange("p k t -> p (k t)"), two_banks(0, 1), ACT.Copy))
                yield 1
                for g in range(4):
                    if g == 2:
                        yield 1
                    said_by(act, "dve", prep, f"m{g}")
                    for j in range(4):
                        i = act.activation(s_p[g % 2][:, j], s_p[g % 2][:, j], ACT.Exp,
                                           bias=mx[:, 0, 4 * g + j:4 * g + j + 1],
                                           accum_out=mx[:, 2, 4 * g + j:4 * g + j + 1])
                        if j < 3:
                            step.mark(i)
                    step.settle()
                    say(i)
                    said_by(act, "pe", prep, f"pT{g}")
                    if g >= 2:
                        said_by(act, "pe", prep, f"o{g - 2}")
                    say(act.activation(s_pT[g % 2].rearrange("p k t -> p (k t)"), two_banks(2, 3), ACT.Copy))
                say(act.activation(mx[:, 1, :], mx[:, 1, :], ACT.Exp))
                turned(prep, "oT")
                yield 1
                yield from select(prep)

            def select(prep):
                yield 1
                said_by(act, "dve", prep, "x2")
                say(act.activation(junk, xc[:], ACT.Square, accum_out=stat[:, 0, 0:1]))
                sqrt(prep, 1, "var2")
                turned(prep, "h2T")
                yield 1
                said_by(act, "pe", prep, "pq0")
                step(act.activation(pqT[:, 0:4, :], ps[:, 2, :].rearrange("p (h t) -> p h t", h=4), ACT.Copy))
                said_by(act, "pe", prep, "pq1")
                say(act.activation(pqT[:, 4:8, :], ps[:, 3, :].rearrange("p (h t) -> p h t", h=4), ACT.Copy))
                yield 1
                yield 1
                yield 1
                yield 1
                said_by(act, "dve", prep, "gshift")
                say(act.activation(ef[:, 1], ef[:, 0], ACT.Exp))
                yield 2

            def preps(prep):
                return gla(prep) if prep.kind == "gla" else swa(prep)

            def rounds(s, lo, n):
                def one(r):
                    for i in range(SLOTS):
                        at = (s * ROUNDS + r) * SLOTS + i
                        act.wait_ge(dotted, at + 1)
                        act.activation(gelu[:, i:i + 1], dots[:, i:i + 1], ACT.Gelu).then_inc(gelued, 1)
                        act.wait_ge(gelued, at + 1)
                        col = (s * ROUNDS + r) * SLOTS + (i - layer[0] * BLOCKS * PICKS)
                        act.activation(coef[:, i:i + 1], gate[:, bass.ds(col, 1)], ACT.Copy,
                                       scale=gelu[:, i:i + 1]).then_inc(weighed, 1)
                        act.wait_ge(weighed, at + 1)
                        if i >= 4:
                            act.wait_ge(used[i - 4], s * ROUNDS + r + 2)
                        else:
                            act.wait_ge(used[i + 4], s * ROUNDS + r + 1)
                        act.activation(diag[:, i % 4, :], ident[:], ACT.Copy,
                                       scale=coef[:, i:i + 1]).then_inc(diag_ready, 1)
                if n == 1:
                    one(lo)
                else:
                    with act.Fori(lo, lo + n) as r:
                        one(r)

            def close(s):
                act.wait_ge(used[SLOTS - 1], s * ROUNDS + (ROUNDS + 1))
                if not (isinstance(s, int) and s == 0):
                    act.wait_ge(stored, s * 16)
                for b in range(2):
                    act.activation(y_sb[:, b * 512:(b + 1) * 512], acc[:, b * 512:(b + 1) * 512],
                                   ACT.Copy).then_inc(acc_taken, 1)

            def stage(s, prep):
                lo = 0
                if prep is not None:
                    for n in preps(prep):
                        rounds(s, lo, n)
                        lo += n
                if lo < ROUNDS:
                    rounds(s, lo, ROUNDS - lo)
                close(s)

            act.wait_ge(consts_dve, 1)
            for dst, w in ((sinb, 1), (cosb, 2)):
                act.activation(dst[:], angle[:, w].rearrange("p b j -> p (b j)"), ACT.Sin).then_inc(consts_act, 1)
            layer = [0]
            for _ in preps(Prep("gla", 0)):
                pass
            with act.Fori(0, BLOCKS - 1) as s:
                stage(s, Prep("gla", s + 1))
            stage(BLOCKS - 1, Prep("swa", 0))
            layer[0] = 1
            with act.Fori(BLOCKS, STAGES - 1) as s:
                stage(s, Prep("swa", s - (BLOCKS - 1)))
            stage(STAGES - 1, None)

        @block.tensor
        def _(pe):
            def say(ins):
                ins.then_inc(said["pe"], 1)

            def turn(src, at=0):
                for k in range(KT):
                    i = pe.transpose(ps[:, at + k // 4, (k % 4) * P:(k % 4 + 1) * P], src[:, k, :], ident[:])
                say(i)

            def strip(prep, n):
                if n < RESIDENT:
                    if isinstance(prep.p, int):
                        pe.wait_ge(res_loaded[n], 16 * (prep.layer + 1))
                else:
                    pe.wait_ge(slot_loaded[(n - RESIDENT) % 2], prep.slot_uses(n - RESIDENT) * 16)
                return weight(prep, n)

            def free(n, ins):
                if n >= RESIDENT:
                    ins.then_inc(strip_used, 1)
                return ins

            def left(prep, n0, bank, event, wait=None):
                for n in range(2):
                    w = strip(prep, n0 + n)
                    for c in range(2):
                        for k in range(KT):
                            i = pe.matmul(ps[:, bank, (2 * n + c) * P:(2 * n + c + 1) * P],
                                          w[:, k, c * P:(c + 1) * P], actT[:, k, :], start=(k == 0),
                                          stop=(k == KT - 1))
                    if n == 0 and n0 + n >= RESIDENT:
                        used_up(i)
                return i

            def right(prep, n, dst, bias=None):
                w = strip(prep, n)
                if bias is not None:
                    pe.matmul(dst, ones[0:1, :], bias, start=True, stop=False)
                for k in range(KT):
                    i = pe.matmul(dst, actT[:, k, :], w[:, k, :], start=(k == 0 and bias is None),
                                  stop=(k == KT - 1))
                return i

            def normed(prep):
                said_by(pe, "dve", prep, "h")
                if not (isinstance(prep.p, int) and prep.layer == 0):
                    said_by(pe, "dve", before(prep), "experts")
                turn(hn)
                said_by(pe, "act", prep, "hT")

            def gla(prep):
                normed(prep)
                say(left(prep, 0, 2, "q"))
                yield 1
                for k in range(KT):
                    i = pe.matmul(ps[0:RANK, 4, 0:P], wlr[:, k, :], actT[:, k, :], start=(k == 0), stop=(k == KT - 1))
                say(i)
                say(left(prep, 2, 3, "k"))
                said_by(pe, "act", prep, "lr")
                pe.wait_ge(small_loaded, (prep.p + prep.layer * BLOCKS) * 16 + 16)
                for h in range(HEADS_A):
                    i = pe.matmul(ps[:, 5, h * P:(h + 1) * P], walpha[:, h * DK:(h + 1) * DK], lrT[:], start=True,
                                  stop=True)
                say(i)
                yield 1
                for n in range(4):
                    i = right(prep, 4 + n, two_banks(0, 1)[:, n * STRIP:(n + 1) * STRIP])
                    if 4 + n >= RESIDENT and n < 3:
                        used_up(i)
                say(i)
                yield 1
                said_by(pe, "dve", prep, "qd")
                for h in range(HEADS_A):
                    i = pe.matmul(ps[:, 4, h * P:(h + 1) * P], g_kinv[:, h], g_qd[:, h], start=True, stop=True)
                say(i)
                said_by(pe, "dve", prep, "kf")
                for h in range(HEADS_A):
                    i = pe.transpose(ps[:, 5, h * P:(h + 1) * P], g_kf[:, h], ident[:])
                say(i)
                for n in range(2):
                    used_up(right(prep, 8 + n, two_banks(2, 3)[:, n * STRIP:(n + 1) * STRIP]))
                yield 1
                used_up(right(prep, 10, two_banks(2, 3)[:, 2 * STRIP:3 * STRIP]))
                say(right(prep, 11, two_banks(2, 3)[:, 3 * STRIP:4 * STRIP]))
                said_by(pe, "act", prep, "kf")
                said_by(pe, "dve", prep, "attn")
                for c in range(2):
                    rows = slice(c * CHUNK, (c + 1) * CHUNK)
                    for h in range(HEADS_A):
                        i = pe.matmul(two_banks(4 * c, 4 * c + 1)[:, h * DV:(h + 1) * DV], g_kft[rows, h, :],
                                      g_v[rows, h, :], start=True, stop=True)
                say(i)
                yield 1
                said_by(pe, "act", prep, "silu")
                said_by(pe, "dve", prep, "state0")
                for h in range(HEADS_A):
                    o = two_banks(2, 3)[:, h * DV:(h + 1) * DV]
                    pe.matmul(o, attnT[:, h], g_v[:, h], start=True, stop=True)
                    pe.matmul(o[0:CHUNK], g_qd[:, h, 0:CHUNK], state0[:, h], start=False, stop=True,
                              skip_group_check=True)
                    i = pe.matmul(o[CHUNK:P], g_qd[:, h, CHUNK:P], state1[:, h], start=False, stop=True,
                                  skip_group_check=True)
                say(i)
                said_by(pe, "dve", prep, "o")
                turn(g_o.rearrange("p h (a t) -> p (h a) t", t=P))
                yield 1
                yield from select(prep)

            def swa(prep):
                normed(prep)
                yield 1
                pe.wait_ge(small_loaded, (prep.p + prep.layer * BLOCKS) * 16 + 16)
                for n in range(4):
                    i = right(prep, n, two_banks(0, 1)[:, n * STRIP:(n + 1) * STRIP],
                              bias_in[:, n * STRIP:(n + 1) * STRIP])
                say(i)
                yield 1
                say(right(prep, 4, ps[:, 2, 0:STRIP], bias_in[:, 4 * STRIP:5 * STRIP]))
                yield 1
                said_by(pe, "dve", prep, "qk")
                for h in range(HEADS_KV):
                    pe.transpose(ps[:, 2, h * P:(h + 1) * P], s_kdup[:, h].rearrange("p a d -> p (a d)"), ident[:])
                turn(s_qk[:, 0:HEADS_Q].rearrange("p (k a) d -> p k (a d)", a=2))
                yield 1
                said_by(pe, "act", prep, "qT")
                for g in range(4):
                    if g == 2:
                        yield 1
                    if g >= 1:
                        said_by(pe, "dve", prep, f"m{g - 1}")
                    for j in range(2):
                        for par in range(2):
                            i = pe.matmul(ps[:, par, j * 2 * P:(j + 1) * 2 * P],
                                          s_qT[par * HD:(par + 1) * HD, 2 * g + j, :],
                                          kT[par * HD:(par + 1) * HD, g // 2, :], start=True, stop=True)
                    say(i)
                    said_by(pe, "act", prep, f"p{g}")
                    if g >= 1:
                        said_by(pe, "act", prep, f"pT{g - 1}")
                    for j in range(4):
                        for b in range(2):
                            m = 2 * j + b
                            i = pe.transpose(ps[:, 2 + m // 4, (m % 4) * P:(m % 4 + 1) * P],
                                             s_p[g % 2][:, j, b * P:(b + 1) * P], ident[:])
                    say(i)
                    said_by(pe, "act", prep, f"pT{g}")
                    for par in range(2):
                        for j in range(2):
                            h = 4 * g + 2 * j + par
                            for b in range(2):
                                i = pe.matmul(two_banks(4, 5)[:, h * HD:(h + 1) * HD],
                                              s_pT[g % 2][:, 2 * (2 * par + j) + b, :],
                                              vv[:, b, (g // 2) * HD:(g // 2 + 1) * HD],
                                              start=(b == 0), stop=(b == 1))
                    say(i)
                said_by(pe, "dve", prep, "o")
                turn(s_o.rearrange("p (k a) d -> p k (a d)", a=2))
                yield 1
                yield from select(prep)

            def used_up(ins):
                ins.then_inc(strip_used, 1)

            def select(prep):
                said_by(pe, "act", prep, "oT")
                n0 = out0(prep)
                for n in range(4):
                    bias = bias_out[:, n * STRIP:(n + 1) * STRIP] if prep.layer else None
                    if prep.layer and n == 0:
                        pe.wait_ge(bias_loaded, prep.p * 16 + 16)
                    i = right(prep, n0 + n, two_banks(4, 5)[:, n * STRIP:(n + 1) * STRIP], bias)
                    if n0 + n >= RESIDENT and n < 3:
                        used_up(i)
                say(i)
                yield 1
                said_by(pe, "dve", prep, "h2")
                turn(h_next[:].rearrange("p (k t) -> p k t", k=KT))
                yield 1
                said_by(pe, "act", prep, "h2T")
                for b in range(2):
                    i = left(prep, pq0(prep) + 2 * b, 2 + b, "pq")
                    say(i)
                said_by(pe, "act", prep, "pq")
                pe.wait_ge(keys_loaded, 16 * (prep.layer + 1))
                for h in range(HEADS_P):
                    for half in range(2):
                        rows = slice(half * HALF, (half + 1) * HALF)
                        i = pe.matmul(ps[:, 4 * half + h // 4, (h % 4) * KEYS:(h % 4 + 1) * KEYS],
                                      pqT[rows, h, :], keysT[rows, h, :], start=True, stop=True)
                say(i)
                yield 1
                yield 1
                yield 1
                yield 1
                yield 2

            def preps(prep):
                return gla(prep) if prep.kind == "gla" else swa(prep)

            def rounds(s, lo, n):
                def one(r):
                    for i in range(SLOTS):
                        pe.wait_ge(diag_ready, (s * ROUNDS + r) * SLOTS + (i + 1))
                        for b in range(2):
                            m = pe.matmul(acc[:, b * 512:(b + 1) * 512], diag[:, i % 4, :],
                                          ring[:, i, D + b * 512:D + (b + 1) * 512], start=False, stop=True,
                                          skip_group_check=True)
                        m.then_inc(used[i], 1)
                if n == 1:
                    one(lo)
                else:
                    with pe.Fori(lo, lo + n) as r:
                        one(r)

            def seed(s, prep):
                if not (isinstance(s, int) and s == 0):
                    pe.wait_ge(acc_taken, s * 2)
                said_by(pe, "dve", prep, "x2")
                for b in range(2):
                    m = pe.matmul(acc[:, b * 512:(b + 1) * 512], ident[:], xc[:, b * 512:(b + 1) * 512],
                                  start=True, stop=True)
                m.then_inc(seeded, 1)

            def stage(s, mine, prep):
                seed(s, mine)
                lo = 0
                if prep is not None:
                    for n in preps(prep):
                        rounds(s, lo, n)
                        lo += n
                if lo < ROUNDS:
                    rounds(s, lo, ROUNDS - lo)

            pe.wait_ge(consts_made, N_CONST_MADE)
            pe.wait_ge(consts_loaded, 16 * N_CONST_LOADS)
            for _ in preps(Prep("gla", 0)):
                pass
            with pe.Fori(0, BLOCKS - 1) as s:
                stage(s, Prep("gla", s), Prep("gla", s + 1))
            stage(BLOCKS - 1, Prep("gla", BLOCKS - 1), Prep("swa", 0))
            with pe.Fori(BLOCKS, STAGES - 1) as s:
                stage(s, Prep("swa", s - BLOCKS), Prep("swa", s - (BLOCKS - 1)))
            stage(STAGES - 1, Prep("swa", BLOCKS - 1), None)


def in_strips(w):
    n = w.shape[1] // STRIP
    return w.reshape(KT, P, n, STRIP).transpose(2, 1, 0, 3).reshape(n, P, KT * STRIP)


def kernel(x, positions, ln_mix, ln_ffn, gla_w_in, gla_w_alpha, gla_b_alpha, gla_norm, gla_w_out, swa_w_in, swa_b_in,
           swa_q_norm, swa_k_norm, swa_sinks, swa_w_out, swa_b_out, peer_w_q, peer_keys, peer_u, peer_v):
    from concourse import bacc
    from concourse.bass_utils import run_bass_kernel_spmd

    a = {k: np.asarray(v) for k, v in dict(
        x=x, positions=positions, ln_mix=ln_mix, ln_ffn=ln_ffn, w_in=gla_w_in, w_alpha=gla_w_alpha,
        b_alpha=gla_b_alpha, norm=gla_norm, w_out=gla_w_out, sw_in=swa_w_in, sb_in=swa_b_in, qn=swa_q_norm,
        kn=swa_k_norm, sinks=swa_sinks, sw_out=swa_w_out, sb_out=swa_b_out, wq=peer_w_q, keys=peer_keys,
        u=peer_u, v=peer_v).items()}
    wide = HEADS_A * (2 * DK + 2 * DV)
    keys = a["keys"].transpose(0, 2, 4, 1, 3).reshape(2, P, HEADS_P, KEYS)
    arrays = {
        "in_x": a["x"][0],
        "in_positions": a["positions"][0].reshape(BLOCKS, P).T,
        "in_gain_mix": a["ln_mix"].reshape(2, KT, P).transpose(2, 0, 1),
        "in_gain_ffn": a["ln_ffn"],
        "in_strips0": np.concatenate([in_strips(w) for w in (a["w_in"][0][:, :wide], a["w_out"][0], a["wq"][0])]),
        "in_strips1": np.concatenate([in_strips(w) for w in (a["sw_in"][0], a["sw_out"][0], a["wq"][1])]),
        "in_w_lr": a["w_in"][0][:, wide:].reshape(KT, P, RANK).transpose(1, 0, 2),
        "in_w_alpha": a["w_alpha"][0],
        "in_b_alpha": a["b_alpha"][0].reshape(HEADS_A, DK).T,
        "in_gla_gain": a["norm"][0].reshape(KT, P).T,
        "in_b_in": a["sb_in"],
        "in_b_out": a["sb_out"],
        "in_qk_gain": np.concatenate([a["qn"], a["kn"]], axis=1),
        "in_sinks": a["sinks"],
        "in_keys0": keys[0],
        "in_keys1": keys[1],
        "in_uv0": np.concatenate([a["u"][0], a["v"][0]], axis=1),
        "in_uv1": np.concatenate([a["u"][1], a["v"][1]], axis=1),
    }
    arrays = {k: np.ascontiguousarray(v) for k, v in arrays.items()}
    nc = bacc.Bacc("TRN2", target_bir_lowering=False, num_devices=1)
    args = [nc.dram_tensor(k, v.shape, mybir.dt.from_np(v.dtype), kind="ExternalInput").ap()
            for k, v in arrays.items()]
    out = nc.dram_tensor("out_0", [SEQ, D], F32, kind="ExternalOutput").ap()
    build(nc, *args, out)
    r = run_bass_kernel_spmd(nc, [arrays], core_ids=[0])
    return r.results[0]["out_0"].reshape(1, SEQ, D)
```

```python
from contextlib import ExitStack

import numpy as np

import concourse.bass as bass
from concourse import mybir

F32 = mybir.dt.float32
U32 = mybir.dt.uint32
I32 = mybir.dt.int32
ALU = mybir.AluOpType
ACT = mybir.ActivationFunctionType
AX = mybir.AxisListType.X

P = 128
D = 1024
SEQ = 512
BLOCKS = SEQ // P
KT = D // P
EPS = 1e-6

HEADS_A, DK, DV, CHUNK, RANK, TAU = 4, 128, 256, 64, 16, 16.0
HEADS_Q, HEADS_KV, HD, WINDOW = 16, 2, 64, 128
GROUP = HEADS_Q // HEADS_KV
ROPE_HALF = HD // 4 // 2
THETA = 500000.0

HEADS_P, KEYS, HALF, TOPK = 8, 128, 64, 16
EXPERTS = KEYS * KEYS
PICKS = HEADS_P * TOPK
SLOTS = 8
ROUNDS = PICKS // SLOTS
STAGES = 2 * BLOCKS

STRIP = 256
STRIPS = (20, 13)
RESIDENT = 6
STREAMED = tuple(s - RESIDENT for s in STRIPS)
FREED = ([None, "v", None, None, None, "r", None, None, None, "y", None, "pq0", None, "pq1"],
         [None, None, "y", None, "pq0", None, "pq1"])
BEAT = 2
BEATS = PICKS // BEAT
SELECT_AT = {"out0": 36, "out1": 37, "out2": 39, "out3": 40, "x2": 42, "var2": 43, "h2": 44, "h2T": 45,
             "pq0": 47, "pq1": 48, "pqa": 50, "sca": 51, "pq2": 51, "pq3": 52, "pqb": 54, "scb": 55,
             "topa": 52, "cana": 54, "keya": 56, "topb": 58, "canb": 60, "keyb": 62}
AT = {
    "gla": {"var": 1, "h": 2, "hT": 3, "q0": 5, "lr": 6, "q1": 6, "k0": 8, "k1": 9, "alpha": 8, "absx": 9, "ln": 10,
            "b": 10, "decay": 11, "qd": 12, "v0": 11, "v1": 12, "v2": 14, "v3": 15, "v": 17, "attn": 17, "mask": 18,
            "r0": 18, "r1": 20, "r2": 21, "r3": 23, "silu": 24, "upd": 24, "state0": 26, "o0": 27, "o1": 28,
            "state1": 30, "osqrt": 30, "o": 31, "oT": 33, **SELECT_AT},
    "swa": {"var": 1, "h": 2, "hT": 3, "q0": 5, "q1": 6, "q2": 8, "q3": 9, "kv": 11, "qsq": 12, "qvar": 13,
            "qn": 14, "rope": 15, "qT": 17, **{f"g{g}": 18 + 4 * g for g in range(4)}, "o": 34, "oT": 35,
            **SELECT_AT},
}
LOWEST = -3.0e38
HIDDEN = -1e30

SELECT = {
    "pe": ["h2T", "pq0", "scores0", "pq1", "scores1"],
    "act": ["sq2", "sqrt2", "h2T", "pq0", "pq1", "gexp0", "gexp1"],
    "dve": ["x2", "var2", "h2", "gshift0", "experts0", "gshift1", "experts1"],
}
EVENTS = {
    "gla": {
        "pe": ["hT", "q", "lr", "k", "alpha", "v", "attn", "kfT", "r", "upd", "o", "oT", "y"] + SELECT["pe"],
        "act": ["sq", "sqrt", "hT", "lr", "exp", "ln", "decay", "v", "kf", "silu", "osq", "osqrt", "oT"]
               + SELECT["act"],
        "dve": ["var", "h", "absx", "bdiff", "qd", "kf", "attn", "state0", "state1", "ovar", "o"] + SELECT["dve"],
    },
    "swa": {
        "pe": ["hT", "q", "kv", "qT"] + [f"{w}{g}" for g in range(4) for w in ("s", "pT", "o")]
              + ["oT", "y"] + SELECT["pe"],
        "act": ["sq", "sqrt", "hT", "qsq", "qsqrt", "kprev", "qT"] + [f"{w}{g}" for g in range(4) for w in ("p", "pT")]
               + ["den", "oT"] + SELECT["act"],
        "dve": ["var", "h", "qvar", "v", "qk"] + [f"m{g}" for g in range(4)] + ["o"] + SELECT["dve"],
    },
}


class Prep:

    def __init__(self, kind, p):
        self.kind, self.p = kind, p
        self.layer = 0 if kind == "gla" else 1

    def value(self, engine, event):
        names = EVENTS[self.kind][engine]
        base = 0 if self.kind == "gla" else BLOCKS * len(EVENTS["gla"][engine])
        return self.p * len(names) + (base + names.index(event) + 1)

    def strips_used(self, n):
        per = [f.count(None) for f in FREED]
        before = 0 if self.layer == 0 else BLOCKS * per[0]
        return self.p * per[self.layer] + (before + FREED[self.layer][:n + 1].count(None))

    def slot_uses(self, n):
        slot = n % 2
        per = [(STREAMED[l] + 1 - slot) // 2 for l in (0, 1)]
        return self.p * per[self.layer] + (n // 2 + 1 + (0 if self.layer == 0 else BLOCKS * per[0]))


def alone(eng, passed):
    eng.sem_inc(passed, 1)


class Steps:

    def __init__(self, eng, sem, passed):
        self.eng, self.sem, self.passed, self.n = eng, sem, passed, 0

    def restart(self):
        alone(self.eng, self.passed)
        self.eng.sem_clear(self.sem)
        self.n = 0

    def mark(self, ins):
        self.n += 1
        ins.then_inc(self.sem, 1)

    def settle(self):
        self.eng.wait_ge(self.sem, self.n)

    def __call__(self, ins):
        self.mark(ins)
        self.settle()


def build(nc, x, positions, gain_mix, gain_ffn, strips0, strips1, w_lr, w_alpha, b_alpha, gla_gain,
          b_in, b_out, qk_gain, sinks, keys0, keys1, uv0, uv1, out):
    strips = (strips0, strips1)
    tables = (uv0, uv1)
    h1 = nc.dram_tensor("h1", [SEQ, D], F32, kind="Internal").ap()

    with ExitStack() as ctx:
        def sb(name, shape, dt=F32):
            return ctx.enter_context(nc.sbuf_tensor(name, shape, dt))

        def sem(name):
            return ctx.enter_context(nc.semaphore(name))

        ring = sb("ring", [P, SLOTS, 2 * D])
        pick_now = sb("pick_now", [P, 2, SLOTS], U32)
        pick = sb("pick", [P, BLOCKS * PICKS], U32)
        gate = sb("gate", [P, BLOCKS * PICKS])
        h_now = sb("h_now", [P, D])
        dots = sb("dots", [P, SLOTS])
        gelu = sb("gelu", [P, SLOTS])
        coef = sb("coef", [P, SLOTS])
        diag = sb("diag", [P, 4, P])
        y_sb = sb("y_sb", [P, D])
        resident = sb("resident", [P, RESIDENT, KT, STRIP])
        stream = sb("stream", [P, 2, KT, STRIP])
        arena = sb("arena", [P, 8192])
        xc = sb("xc", [P, D])
        h_next = sb("h_next", [P, D])
        actT = sb("actT", [P, KT, P])
        past = sb("past", [P, 2 * D])
        attnT = sb("attnT", [P, HEADS_A, P])
        keysT = sb("keysT", [P, HEADS_P, KEYS])
        ident = sb("ident", [P, P])
        causal = sb("causal", [P, P])
        band = sb("band", [P, 2 * P])
        ones = sb("ones", [1, P])
        scan_keep = sb("scan_keep", [P, HEADS_A * P])
        iota16 = sb("iota16", [P, TOPK])
        gmix = sb("gmix", [P, 2, KT])
        wlr = sb("wlr", [P, KT, RANK])
        balpha = sb("balpha", [P, HEADS_A])
        ggla = sb("ggla", [P, KT])
        lrT = sb("lrT", [RANK, P])
        gqk = sb("gqk", [P, 2, HD])
        sink = sb("sink", [P, HEADS_Q])
        posi = sb("posi", [P, BLOCKS], I32)
        posf = sb("posf", [P, BLOCKS])
        invf = sb("invf", [P, ROPE_HALF])
        cosb = sb("cosb", [P, BLOCKS * ROPE_HALF])
        sinb = sb("sinb", [P, BLOCKS * ROPE_HALF])
        rope_now = sb("rope_now", [P, 2, ROPE_HALF])
        stat = sb("stat", [P, 6, 24])
        mx = sb("mx", [P, 3, HEADS_Q])

        acc = ctx.enter_context(nc.psum_tensor("acc", [P, D], F32))
        ps = ctx.enter_context(nc.psum_tensor("ps", [P, 6, 512], F32))

        got = [sem(f"got{s}") for s in range(SLOTS)]
        used = [sem(f"used{s}") for s in range(SLOTS)]
        picks_copied = sem("picks_copied")
        started = sem("started")
        dotted = sem("dotted")
        gelued = sem("gelued")
        weighed = sem("weighed")
        diag_ready = sem("diag_ready")
        seeded = sem("seeded")
        acc_taken = sem("acc_taken")
        stored = sem("stored")
        h_taken = sem("h_taken")
        said = {"pe": sem("pe_said"), "act": sem("act_said"), "dve": sem("dve_said")}
        own = {"pe": sem("pe_step"), "act": sem("act_step"), "dve": sem("dve_step"), "pool": sem("pool_step")}
        passed = {e: sem(e + "_passed") for e in own}
        x_loaded = sem("x_loaded")
        gain_loaded = sem("gain_loaded")
        small_loaded = sem("small_loaded")
        bias_loaded = sem("bias_loaded")
        res_loaded = [sem(f"res_loaded{i}") for i in range(RESIDENT)]
        slot_loaded = [sem(f"slot_loaded{i}") for i in range(2)]
        strip_used = sem("strip_used")
        consts_loaded = sem("consts_loaded")
        keys_loaded = sem("keys_loaded")
        consts_made = sem("consts_made")
        consts_act = sem("consts_act")
        consts_dve = sem("consts_dve")
        band_made = sem("band_made")

        N_CONST_LOADS = 7
        N_CONST_MADE = 15

        def area(lo, *dims):
            n = int(np.prod(dims))
            v = arena[:, lo:lo + n]
            if len(dims) == 2:
                return v.rearrange("p (a b) -> p a b", a=dims[0])
            if len(dims) == 3:
                return v.rearrange("p (a b c) -> p a b c", a=dims[0], b=dims[1])
            return v

        g_v = area(0, HEADS_A, DV)
        g_r = area(1024, HEADS_A, DV)
        g_o = area(2048, HEADS_A, DV)
        hn = area(3072, KT, P)
        angle = area(7680, 4, BLOCKS, ROPE_HALF)
        g_b = area(4096, HEADS_A, P)
        g_t = area(4608, HEADS_A, P)
        g_eb = area(5120, HEADS_A, P)
        g_enb = area(5632, HEADS_A, P)
        g_ef = area(6144, HEADS_A, P)
        g_qd = area(6656, HEADS_A, P)
        g_kinv = area(7168, HEADS_A, P)
        g_kf = area(7680, HEADS_A, P)
        walpha = arena[0:RANK, 6656:7168]
        g_kft = area(4096, HEADS_A, DK)
        junk = area(2048, D)
        ffn_gain = area(5120, D)
        s_qk = area(0, HEADS_Q + HEADS_KV, HD)
        s_sq = area(1152, HEADS_Q + HEADS_KV, HD)
        s_qT = area(1152, KT, P)
        s_p = [area(2304 + 1024 * i, 4, 2 * P) for i in range(2)]
        s_kdup = area(4352, HEADS_KV, 2, HD)
        s_pT = [area(4352 + 1024 * i, 8, P) for i in range(2)]
        s_o = area(6400, HEADS_Q, HD)
        bias_in = arena[0:1, 4352:5632]
        bias_out = arena[0:1, 4096:5120]
        s_rope = area(7424, 4, HEADS_Q + HEADS_KV, ROPE_HALF)
        pqT = area(0, HEADS_P, P)
        c_rest = area(1024, 4, KEYS)
        cand = area(2048, HEADS_P // 2, TOPK, TOPK)
        cand_rest = area(3072, HEADS_P // 2, TOPK * TOPK)
        onehot = area(4096, HEADS_P // 2 * TOPK, TOPK)
        top = area(6144, 2 * HEADS_P, TOPK)
        topi = area(6400, 2 * HEADS_P, TOPK).bitcast(U32)
        topf = area(6656, 2 * HEADS_P, TOPK)
        best = area(6912, HEADS_P, TOPK)
        besti = area(7040, HEADS_P, TOPK).bitcast(U32)
        ab = area(7168, 2, HEADS_P, TOPK).bitcast(U32)
        abf = area(7424, 2, HEADS_P, TOPK)
        ef = area(7680, 2, HEADS_P, TOPK)
        gsm = area(7936, 2, HEADS_P)

        state0 = past[:, 0:D].rearrange("p (h v) -> p h v", h=HEADS_A)
        state1 = past[:, D:2 * D].rearrange("p (h v) -> p h v", h=HEADS_A)
        kT = past[:, 0:2 * 2 * P].rearrange("p (h t) -> p h t", h=HEADS_KV)
        vv = past[:, D:D + 2 * P].rearrange("p (b n) -> p b n", b=2)

        def two_banks(a, b):
            return ps[:, a:b + 1, :].rearrange("p a n -> p (a n)")

        def said_by(eng, who, prep, event):
            eng.wait_ge(said[who], prep.value(who, event))

        def before(prep):
            if isinstance(prep.p, int) and prep.layer == 1:
                return Prep("gla", BLOCKS - 1)
            return Prep(prep.kind, prep.p - 1)

        def weight(prep, n):
            if n < RESIDENT:
                return resident[:, n]
            return stream[:, (n - RESIDENT) % 2]

        def out0(prep):
            return 12 if prep.layer == 0 else 5

        def pq0(prep):
            return 16 if prep.layer == 0 else 9

        def beside(eng, anchor, half, prep_parts):
            per = SLOTS // BEAT
            done = 0

            def serve(until):
                nonlocal done
                while done < until:
                    r, beat = divmod(done, per)
                    if beat == 0 and until - done >= 2 * per:
                        n = (until - done) // per
                        alone(eng, anchor)
                        with eng.Fori(r, r + n) as rr:
                            half(rr, 0, per)
                        done += n * per
                    else:
                        n = min(per - beat, until - done)
                        half(r, beat, n)
                        done += n

            for beat in prep_parts:
                serve(beat)
            serve(BEATS)

        block = ctx.enter_context(nc.Block())

        @block.sync
        def _(sp):
            for dst, src in ((gmix[:], gain_mix), (wlr[:], w_lr), (balpha[:], b_alpha),
                             (ggla[:], gla_gain),
                             (gqk[:].rearrange("p a d -> p (a d)"), qk_gain.to_broadcast([P, 2 * HD])),
                             (sink[:], sinks.to_broadcast([P, HEADS_Q])), (posi[:], positions)):
                sp.dma_start(dst, src).then_inc(consts_loaded, 16)
            sp.dma_start(keysT[:], keys0).then_inc(keys_loaded, 16)

            def freed(prep, n):
                event = FREED[prep.layer][n]
                if event is None:
                    sp.wait_ge(strip_used, prep.strips_used(n))
                else:
                    said_by(sp, "pe", prep, event)

            def preps(prep):
                first = isinstance(prep.p, int)
                src = x if prep.layer == 0 else h1
                stage = prep.p + BLOCKS * prep.layer
                if not (first and prep.layer == 0):
                    sp.wait_ge(seeded, stage)
                if prep.layer == 1:
                    sp.wait_ge(stored, prep.p * 16 + 17)
                sp.dma_start(xc[:], src[bass.ds(prep.p * P, P), :]).then_inc(x_loaded, 16)
                if not (first and prep.layer == 0):
                    said_by(sp, "dve", before(prep), "experts1")
                if prep.layer == 0:
                    sp.dma_start(walpha, w_alpha).then_inc(small_loaded, 16)
                else:
                    sp.dma_start(bias_in, b_in).then_inc(small_loaded, 16)
                if first and prep.layer == 1:
                    said_by(sp, "pe", Prep("gla", BLOCKS - 1), "scores1")
                    sp.dma_start(keysT[:], keys1).then_inc(keys_loaded, 16)
                if first:
                    for n in range(RESIDENT):
                        sp.dma_start(resident[:, n].rearrange("p k c -> p (k c)"), strips[prep.layer][n])\
                          .then_inc(res_loaded[n], 16)
                for n in range(STREAMED[prep.layer]):
                    if n == STREAMED[prep.layer] - 5:
                        said_by(sp, "pe", prep, "oT")
                        sp.dma_start(ffn_gain, gain_ffn[prep.layer:prep.layer + 1, :].to_broadcast([P, D]))\
                          .then_inc(gain_loaded, 16)
                        if prep.layer == 1:
                            sp.dma_start(bias_out, b_out).then_inc(bias_loaded, 16)
                    if n >= 2:
                        freed(prep, n - 2)
                    elif not (first and prep.layer == 0):
                        last = STREAMED[before(prep).layer] - 1
                        freed(before(prep), last if last % 2 == n else last - 1)
                    sp.dma_start(stream[:, n % 2].rearrange("p k c -> p (k c)"),
                                 strips[prep.layer][RESIDENT + n]).then_inc(slot_loaded[n % 2], 16)

            def close(s, layer):
                sp.wait_ge(acc_taken, s * 2 + 3)
                dst = h1 if layer == 0 else out
                sp.dma_start(dst[bass.ds((s - layer * BLOCKS) * P, P), :], y_sb[:]).then_inc(stored, 16)

            preps(Prep("gla", 0))
            with sp.Fori(0, BLOCKS - 1) as s:
                preps(Prep("gla", s + 1))
                close(s, 0)
            preps(Prep("swa", 0))
            close(BLOCKS - 1, 0)
            with sp.Fori(BLOCKS, STAGES - 1) as s:
                preps(Prep("swa", s - (BLOCKS - 1)))
                close(s, 1)
            close(STAGES - 1, 1)
            sp.wait_ge(stored, 16 * STAGES + 1)

        @block.gpsimd
        def _(pool):
            step = Steps(pool, own["pool"], passed["pool"])
            made = [0]

            def const(ins):
                made[0] += 1
                ins.then_inc(consts_made, 1)
                pool.wait_ge(consts_made, made[0])

            const(pool.memset(ident[:], 0.0))
            const(pool.affine_select(out=ident[:], in_=ident[:], compare_op=ALU.not_equal, fill=1.0, base=0,
                                     pattern=[[-1, P]], channel_multiplier=1))
            const(pool.memset(causal[:], 1.0))
            const(pool.affine_select(out=causal[:], in_=causal[:], compare_op=ALU.is_ge, fill=0.0, base=0,
                                     pattern=[[1, P]], channel_multiplier=-1))
            const(pool.memset(causal[0:CHUNK, CHUNK:P], 0.0))
            const(pool.memset(band[:, 0:P], HIDDEN))
            const(pool.memset(band[:, P:2 * P], 0.0))
            const(pool.affine_select(out=band[:, P:2 * P], in_=band[:, P:2 * P], compare_op=ALU.is_ge, fill=HIDDEN,
                                     base=0, pattern=[[-1, P]], channel_multiplier=1))
            const(pool.memset(ones[:], 1.0))
            const(pool.memset(scan_keep[:], 1.0))
            const(pool.memset(scan_keep[:].rearrange("p (c t) -> p c t", t=CHUNK)[:, :, 0:1], 0.0))
            const(pool.iota(iota16[:], [[1, TOPK]], base=0, channel_multiplier=0,
                            allow_small_or_imprecise_dtypes=True))
            const(pool.memset(attnT[:], 0.0))
            const(pool.memset(past[:], 0.0))
            for j in range(ROPE_HALF):
                f = float(np.float32(THETA) ** np.float32(-2.0 * j / (2 * ROPE_HALF)))
                last = pool.memset(invf[:, j:j + 1], f)
                if j < ROPE_HALF - 1:
                    step(last)
            const(last)
            assert made[0] == N_CONST_MADE
            for i in range(SLOTS):
                pool.memset(pick_now[:, 0, i:i + 1], 0).then_inc(used[i], 1)
            pool.memset(pick_now[:, 1, :], 0).then_inc(started, 1)

            def stage(s, prep, layer):
                for part in range(2):
                    said_by(pool, "dve", prep, f"experts{part}")
                    alone(pool, passed["pool"])
                    base = s * (ROUNDS // 2)
                    with pool.Fori(part * ROUNDS // 4, (part + 1) * ROUNDS // 4) as pair:
                        for half in range(2):
                            n = (base + pair) * 2 + half
                            step.restart()
                            step(pool.tensor_copy(
                                pick_now[:, half, :],
                                pick[:, bass.ds((base + pair) * (2 * SLOTS)
                                                + (half * SLOTS - layer * BLOCKS * PICKS), SLOTS)]))
                            for i in range(SLOTS):
                                pool.wait_ge(used[i], n + 1)
                                alone(pool, passed["pool"])
                                pool.indirect_dma_start(
                                    ring[:, i, :], None, tables[layer],
                                    bass.IndirectOffsetOnAxis(ap=pick_now[:, half, i:i + 1], axis=0),
                                ).then_inc(got[i], 16)

            pool.wait_ge(started, 1)
            with pool.Fori(0, BLOCKS) as s:
                stage(s, Prep("gla", s), 0)
            said_by(pool, "dve", Prep("swa", 0), "experts1")
            step.restart()
            step(pool.memset(band[:, 0:P], 0.0))
            pool.affine_select(out=band[:, 0:P], in_=band[:, 0:P], compare_op=ALU.is_ge, fill=HIDDEN, base=-1,
                               pattern=[[1, P]], channel_multiplier=-1).then_inc(band_made, 1)
            with pool.Fori(BLOCKS, STAGES) as s:
                stage(s, Prep("swa", s - BLOCKS), 1)

        @block.vector
        def _(dve):
            step = Steps(dve, own["dve"], passed["dve"])

            def say(prep, event, ins):
                ins.then_inc(said["dve"], 1)

            def variance(prep, n, scale, event):
                v = stat[:, 1, 0:n]
                say(prep, event, dve.tensor_scalar(v, stat[:, 0, 0:n], scale, EPS, ALU.mult, ALU.add))
                said_by(dve, "dve", prep, event)
                return v

            def root(prep, n, v, sqrt_event):
                r, t, u = stat[:, 3, 0:n], stat[:, 4, 0:n], stat[:, 5, 0:n]
                said_by(dve, "act", prep, sqrt_event)
                step(dve.reciprocal(r, stat[:, 2, 0:n]))
                step(dve.tensor_tensor(t, r, r, ALU.mult))
                step(dve.tensor_tensor(u, t, v, ALU.mult))
                step(dve.tensor_scalar(t, u, -0.5, 1.5, ALU.mult, ALU.add))
                step(dve.tensor_tensor(v, r, t, ALU.mult))
                return v

            def normed(prep, at):
                yield at["var"]
                said_by(dve, "act", prep, "sq")
                v = variance(prep, 1, 1.0 / D, "var")
                yield at["h"]
                r = root(prep, 1, v, "sqrt")
                say(prep, "h", dve.tensor_scalar(hn.rearrange("p k t -> p (k t)"), xc[:], r, None, ALU.mult))

            def gla(prep, at):
                step.restart()
                yield from normed(prep, at)
                yield at["absx"]
                said_by(dve, "pe", prep, "alpha")
                for h in range(HEADS_A):
                    step.mark(dve.tensor_scalar(g_b[:, h], ps[:, 5, h * P:(h + 1) * P], balpha[:, h:h + 1], None,
                                                ALU.add))
                step.settle()
                say(prep, "absx", dve.scalar_tensor_tensor(g_t, g_b, -1.0, g_b, ALU.mult, ALU.max))
                yield at["b"]
                said_by(dve, "act", prep, "ln")
                step(dve.scalar_tensor_tensor(g_b, g_b, 0.0, g_t, ALU.min, ALU.subtract))
                step(dve.tensor_tensor_scan(g_t.rearrange("p h t -> p (h t)"), scan_keep[:],
                                            g_b.rearrange("p h t -> p (h t)"), 0.0, ALU.mult, ALU.add))
                chunks = g_t.rearrange("p h (c t) -> p (h c) t", c=P // CHUNK)
                say(prep, "bdiff", dve.tensor_tensor(
                    g_b.rearrange("p h (c t) -> p (h c) t", c=P // CHUNK),
                    chunks[:, :, CHUNK - 1:CHUNK].to_broadcast([P, HEADS_A * P // CHUNK, CHUNK]), chunks,
                    ALU.subtract))
                yield at["qd"]
                said_by(dve, "act", prep, "decay")
                q, k = ps[:, 2, :].rearrange("p (h t) -> p h t", h=HEADS_A), \
                    ps[:, 3, :].rearrange("p (h t) -> p h t", h=HEADS_A)
                step.mark(dve.scalar_tensor_tensor(g_qd, q, DK ** -0.5, g_eb, ALU.mult, ALU.mult))
                say(prep, "qd", dve.tensor_tensor(g_kinv, k, g_enb, ALU.mult))
                said_by(dve, "dve", prep, "qd")
                step.settle()
                say(prep, "kf", dve.tensor_tensor(g_kf, k, g_ef, ALU.mult))
                yield at["mask"]
                said_by(dve, "pe", prep, "attn")
                alone(dve, passed["dve"])
                say(prep, "attn", dve.copy_predicated(
                    attnT[:], causal[:].bitcast(U32).rearrange("p (o t) -> p o t", o=1).to_broadcast([P, HEADS_A, P]),
                    ps[:, 4, :].rearrange("p (h t) -> p h t", h=HEADS_A)))
                yield at["state0"]
                said_by(dve, "pe", prep, "upd")
                last = g_eb.rearrange("p h (c t) -> p h c t", c=2)
                for h in range(HEADS_A):
                    i = dve.scalar_tensor_tensor(state1[:, h], state0[:, h], last[:, h, 0, CHUNK - 1:CHUNK],
                                                 two_banks(0, 1)[:, h * DV:(h + 1) * DV], ALU.mult, ALU.add)
                    if h < HEADS_A - 1:
                        step.mark(i)
                say(prep, "state0", i)
                said_by(dve, "dve", prep, "state0")
                step.settle()
                yield at["state1"]
                said_by(dve, "pe", prep, "o")
                for h in range(HEADS_A):
                    i = dve.scalar_tensor_tensor(state0[:, h], state1[:, h], last[:, h, 1, CHUNK - 1:CHUNK],
                                                 two_banks(4, 5)[:, h * DV:(h + 1) * DV], ALU.mult, ALU.add)
                    if h < HEADS_A - 1:
                        step.mark(i)
                say(prep, "state1", i)
                said_by(dve, "dve", prep, "state1")
                step.settle()
                said_by(dve, "act", prep, "osq")
                v = variance(prep, HEADS_A, 1.0 / DV, "ovar")
                yield at["o"]
                r = root(prep, HEADS_A, v, "osqrt")
                for h in range(HEADS_A):
                    i = dve.scalar_tensor_tensor(g_o[:, h], two_banks(2, 3)[:, h * DV:(h + 1) * DV], r[:, h:h + 1],
                                                 g_r[:, h], ALU.mult, ALU.mult)
                    if h < HEADS_A - 1:
                        step.mark(i)
                say(prep, "o", i)
                said_by(dve, "dve", prep, "o")
                step.settle()
                yield from select(prep, at)

            def swa(prep, at):
                step.restart()
                yield from normed(prep, at)
                step(dve.tensor_copy(rope_now[:, 0, :], cosb[:, bass.ds(prep.p * ROPE_HALF, ROPE_HALF)]))
                step(dve.tensor_copy(rope_now[:, 1, :], sinb[:, bass.ds(prep.p * ROPE_HALF, ROPE_HALF)]))
                NH = HEADS_Q + HEADS_KV
                yield at["qvar"]
                said_by(dve, "act", prep, "qsq")
                step(dve.tensor_reduce(stat[:, 0, 0:NH], s_sq, AX, ALU.add))
                v = variance(prep, NH, 1.0 / HD, "qvar")
                yield at["qn"]
                r = root(prep, NH, v, "qsqrt")
                rb = r.rearrange("p (h o) -> p h o", o=1)
                q = two_banks(0, 1).rearrange("p (h d) -> p h d", h=HEADS_Q)
                k = ps[:, 2, 0:HEADS_KV * HD].rearrange("p (h d) -> p h d", h=HEADS_KV)
                step.mark(dve.tensor_tensor(s_qk[:, 0:HEADS_Q], q, rb[:, 0:HEADS_Q].to_broadcast([P, HEADS_Q, HD]),
                                            ALU.mult))
                step.mark(dve.tensor_tensor(s_qk[:, HEADS_Q:NH], k,
                                            rb[:, HEADS_Q:NH].to_broadcast([P, HEADS_KV, HD]), ALU.mult))
                step(dve.tensor_copy(vv[:, 0, :], vv[:, 1, :]))
                say(prep, "v", dve.tensor_copy(vv[:, 1, :], ps[:, 2, HEADS_KV * HD:2 * HEADS_KV * HD]))
                step.mark(dve.tensor_tensor(s_qk[:, 0:HEADS_Q], s_qk[:, 0:HEADS_Q],
                                            gqk[:, 0:1, :].to_broadcast([P, HEADS_Q, HD]), ALU.mult))
                step.mark(dve.tensor_tensor(s_qk[:, HEADS_Q:NH], s_qk[:, HEADS_Q:NH],
                                            gqk[:, 1:2, :].to_broadcast([P, HEADS_KV, HD]), ALU.mult))
                step.settle()
                yield at["rope"]
                x1, x2 = s_qk[:, :, 0:ROPE_HALF], s_qk[:, :, ROPE_HALF:2 * ROPE_HALF]
                cb = rope_now[:, 0:1, :].to_broadcast([P, NH, ROPE_HALF])
                sb_ = rope_now[:, 1:2, :].to_broadcast([P, NH, ROPE_HALF])
                for i, (a, b) in enumerate(((x1, cb), (x2, sb_), (x2, cb), (x1, sb_))):
                    step.mark(dve.tensor_tensor(s_rope[:, i], a, b, ALU.mult))
                step.settle()
                step.mark(dve.tensor_tensor(x1, s_rope[:, 0], s_rope[:, 1], ALU.subtract))
                step.mark(dve.tensor_tensor(x2, s_rope[:, 2], s_rope[:, 3], ALU.add))
                step.settle()
                kk = s_qk[:, HEADS_Q:NH]
                step(dve.tensor_copy(s_kdup[:, :, 0, :], kk))
                say(prep, "qk", dve.tensor_copy(s_kdup[:, :, 1, :], kk))
                for g in range(4):
                    yield at[f"g{g}"] + 1
                    if g >= 2:
                        said_by(dve, "pe", prep, f"pT{g - 2}")
                    said_by(dve, "pe", prep, f"s{g}")
                    sc = ps[:, 0:2, :].rearrange("p b (h t) -> p (b h) t", h=2)
                    step(dve.scalar_tensor_tensor(
                        s_p[g % 2], sc, HD ** -0.5,
                        band[:].rearrange("p (o t) -> p o t", o=1).to_broadcast([P, 4, 2 * P]), ALU.mult, ALU.add))
                    m = mx[:, 0, 4 * g:4 * g + 4]
                    step(dve.tensor_reduce(m, s_p[g % 2], AX, ALU.max))
                    for par in range(2):
                        step.mark(dve.tensor_tensor(m[:, 2 * par:2 * par + 2], m[:, 2 * par:2 * par + 2],
                                                    sink[:, 4 * g + par:4 * g + 4:2], ALU.max))
                    step.settle()
                    for par in range(2):
                        step.mark(dve.tensor_tensor(mx[:, 1, 4 * g + 2 * par:4 * g + 2 * par + 2],
                                                    sink[:, 4 * g + par:4 * g + 4:2], m[:, 2 * par:2 * par + 2],
                                                    ALU.subtract))
                    step.settle()
                    say(prep, f"m{g}", dve.tensor_scalar(m, m, -1.0, None, ALU.mult))
                yield at["o"]
                said_by(dve, "act", prep, "den")
                step(dve.tensor_tensor(stat[:, 4, 0:HEADS_Q], mx[:, 1, :], mx[:, 2, :], ALU.add))
                step(dve.reciprocal(stat[:, 5, 0:HEADS_Q], stat[:, 4, 0:HEADS_Q]))
                said_by(dve, "pe", prep, "o3")
                rd = stat[:, 5, 0:HEADS_Q].rearrange("p (g a b o) -> p g a b o", g=4, a=2, o=1)
                oo = s_o.rearrange("p (g b a) d -> p g b a d", g=4, a=2)
                pp = two_banks(4, 5).rearrange("p (g b a d) -> p g b a d", g=4, b=2, a=2)
                for g in range(4):
                    for par in range(2):
                        i = dve.tensor_tensor(oo[:, g, :, par, :], pp[:, g, :, par, :],
                                              rd[:, g, par].to_broadcast([P, 2, HD]), ALU.mult)
                        if (g, par) != (3, 1):
                            step.mark(i)
                step.settle()
                say(prep, "o", i)
                said_by(dve, "dve", prep, "o")
                yield from select(prep, at)

            def select(prep, at):
                yield at["x2"]
                said_by(dve, "pe", prep, "y")
                for b in range(2):
                    i = dve.tensor_tensor(xc[:, b * 512:(b + 1) * 512], xc[:, b * 512:(b + 1) * 512],
                                          ps[:, 4 + b, :], ALU.add)
                    if b == 0:
                        step.mark(i)
                say(prep, "x2", i)
                said_by(dve, "dve", prep, "x2")
                step.settle()
                yield at["var2"]
                said_by(dve, "act", prep, "sq2")
                v = variance(prep, 1, 1.0 / D, "var2")
                yield at["h2"]
                r = root(prep, 1, v, "sqrt2")
                dve.wait_ge(gain_loaded, (prep.p + prep.layer * BLOCKS) * 16 + 16)
                say(prep, "h2", dve.scalar_tensor_tensor(h_next[:], xc[:], r, ffn_gain, ALU.mult, ALU.mult))
                said_by(dve, "dve", prep, "h2")
                for part in range(2):
                    yield from choose(prep, at, part, range(part * HEADS_P // 2, (part + 1) * HEADS_P // 2))

            def choose(prep, at, part, heads):
                letter = "ab"[part]
                hs = slice(heads[0], heads[-1] + 1)
                n_h = len(heads)

                def score(v):
                    half, h = v // HEADS_P, v % HEADS_P
                    return ps[:, 4 * half + h // 4, (h % 4) * KEYS:(h % 4 + 1) * KEYS]

                yield at["top" + letter]
                said_by(dve, "pe", prep, f"scores{part}")
                alone(dve, passed["dve"])
                for half in range(2):
                    vs = [half * HEADS_P + h for h in heads]
                    for v in vs:
                        step.mark(dve.max(top[:, v, 0:8], score(v)))
                    step.settle()
                    for v in vs:
                        step.mark(dve.max_index(topi[:, v, 0:8], top[:, v, 0:8], score(v)))
                        step.mark(dve.match_replace(c_rest[:, v % 4], top[:, v, 0:8], score(v), LOWEST))
                    step.settle()
                    for v in vs:
                        step.mark(dve.max(top[:, v, 8:16], c_rest[:, v % 4]))
                    step.settle()
                    for v in vs:
                        step.mark(dve.max_index(topi[:, v, 8:16], top[:, v, 8:16], c_rest[:, v % 4]))
                    step.mark(dve.tensor_copy(topf[:, vs[0]:vs[-1] + 1, 0:8], topi[:, vs[0]:vs[-1] + 1, 0:8]))
                    step.settle()
                    step.mark(dve.tensor_copy(topf[:, vs[0]:vs[-1] + 1, 8:16], topi[:, vs[0]:vs[-1] + 1, 8:16]))
                    step.settle()
                    if half == 0:
                        yield at["top" + letter] + 1
                yield at["can" + letter]
                flat = cand.rearrange("p h a b -> p h (a b)")
                for pair in range(2):
                    two = [heads[2 * pair], heads[2 * pair + 1]]
                    for h in two:
                        step.mark(dve.tensor_tensor(
                            cand[:, h % 4],
                            top[:, h, :].rearrange("p (a o) -> p a o", o=1).to_broadcast([P, TOPK, TOPK]),
                            top[:, HEADS_P + h, :].rearrange("p (o b) -> p o b", o=1).to_broadcast([P, TOPK, TOPK]),
                            ALU.add))
                    step.settle()
                    for h in two:
                        step.mark(dve.max(best[:, h, 0:8], flat[:, h % 4]))
                    step.settle()
                    for h in two:
                        step.mark(dve.max_index(besti[:, h, 0:8], best[:, h, 0:8], flat[:, h % 4]))
                        step.mark(dve.match_replace(cand_rest[:, h % 4], best[:, h, 0:8], flat[:, h % 4], LOWEST))
                    step.settle()
                    for h in two:
                        step.mark(dve.max(best[:, h, 8:16], cand_rest[:, h % 4]))
                    step.settle()
                    for h in two:
                        step.mark(dve.max_index(besti[:, h, 8:16], best[:, h, 8:16], cand_rest[:, h % 4]))
                    step.settle()
                    if pair == 0:
                        yield at["can" + letter] + 1
                say(prep, f"gshift{part}", dve.tensor_tensor(
                    ef[:, 0, hs], best[:, hs], best[:, hs, 0:1].to_broadcast([P, n_h, TOPK]), ALU.subtract))
                yield at["key" + letter]
                step.mark(dve.tensor_scalar(ab[:, 0, hs], besti[:, hs], 4, None, ALU.logical_shift_right))
                step.mark(dve.tensor_scalar(ab[:, 1, hs], besti[:, hs], TOPK - 1, None, ALU.bitwise_and))
                step.settle()
                step(dve.tensor_copy(abf[:, :, hs], ab[:, :, hs]))
                said_by(dve, "act", prep, f"gexp{part}")
                step(dve.tensor_reduce(gsm[:, 0, hs], ef[:, 1, hs], AX, ALU.add))
                step(dve.reciprocal(gsm[:, 1, hs], gsm[:, 0, hs]))
                cols = bass.ds(prep.p * PICKS + part * (PICKS // 2), PICKS // 2)
                step(dve.tensor_tensor(
                    gate[:, cols].rearrange("p (h k) -> p h k", h=n_h), ef[:, 1, hs],
                    gsm[:, 1, hs].rearrange("p (h o) -> p h o", o=1).to_broadcast([P, n_h, TOPK]), ALU.mult))
                for half in range(2):
                    for h in heads:
                        step.mark(dve.tensor_tensor(
                            onehot[:, h % 4 * TOPK:(h % 4 + 1) * TOPK, :],
                            abf[:, half, h, :].rearrange("p (k o) -> p k o", o=1).to_broadcast([P, TOPK, TOPK]),
                            iota16[:].rearrange("p (o j) -> p o j", o=1).to_broadcast([P, TOPK, TOPK]),
                            ALU.is_equal))
                    step.settle()
                    for h in heads:
                        o = onehot[:, h % 4 * TOPK:(h % 4 + 1) * TOPK, :]
                        step.mark(dve.tensor_tensor(
                            o, o, topf[:, half * HEADS_P + h, :].rearrange("p (o j) -> p o j", o=1).to_broadcast(
                                [P, TOPK, TOPK]), ALU.mult))
                    step.settle()
                    step(dve.tensor_reduce(ef[:, half, hs].rearrange("p h k -> p (h k)"), onehot, AX,
                                           ALU.add))
                    if half == 0:
                        yield at["key" + letter] + 1
                step(dve.scalar_tensor_tensor(ef[:, 0, hs], ef[:, 0, hs], float(KEYS), ef[:, 1, hs], ALU.mult,
                                              ALU.add))
                say(prep, f"experts{part}", dve.tensor_copy(pick[:, cols],
                                                           ef[:, 0, hs].rearrange("p h k -> p (h k)")))

            def preps(prep):
                return (gla if prep.kind == "gla" else swa)(prep, AT[prep.kind])

            def take_h(s):
                dve.wait_ge(dotted, s * PICKS + 1)
                dve.tensor_copy(h_now[:], h_next[:]).then_inc(h_taken, 1)
                dve.wait_ge(h_taken, s + 1)

            def serve(s):
                def part(r, beat, n):
                    for i in range(beat * BEAT, (beat + n) * BEAT):
                        dve.wait_ge(got[i], (s * ROUNDS + r) * 16 + 16)
                        dve.tensor_tensor_reduce(ring[:, i, 0:D], ring[:, i, 0:D], h_now[:], 1.0, 0.0, ALU.mult,
                                                 ALU.add, dots[:, i:i + 1]).then_inc(dotted, 1)
                return part

            dve.wait_ge(consts_made, N_CONST_MADE)
            dve.wait_ge(consts_loaded, 16 * N_CONST_LOADS)
            step.restart()
            step(dve.tensor_copy(posf[:], posi[:]))
            for b in range(BLOCKS):
                step.mark(dve.tensor_scalar(angle[:, 0, b, :], invf[:], posf[:, b:b + 1], None, ALU.mult))
            step.settle()
            TWO_PI = 2.0 * np.pi
            c1 = 6.28125
            c2 = float(np.float32(TWO_PI - c1) - np.float32(TWO_PI - c1) % np.float32(2.0 ** -20))
            c3 = float(TWO_PI - c1 - c2)
            ROUND = 1.5 * 2.0 ** 23
            PI = 3.1415925
            for w, turn in ((1, 0.0), (2, 0.25)):
                a, k = angle[:, w], angle[:, 3]
                step(dve.tensor_scalar(k, angle[:, 0], 1.0 / TWO_PI, turn, ALU.mult, ALU.add))
                step(dve.tensor_scalar(k, k, ROUND, None, ALU.add))
                step(dve.tensor_scalar(k, k, ROUND, None, ALU.subtract))
                step(dve.scalar_tensor_tensor(a, k, -c1, angle[:, 0], ALU.mult, ALU.add))
                step(dve.scalar_tensor_tensor(a, k, -c2, a, ALU.mult, ALU.add))
                step(dve.scalar_tensor_tensor(a, k, -c3, a, ALU.mult, ALU.add))
                step(dve.tensor_scalar(a, a, turn * TWO_PI, PI, ALU.add, ALU.min))
                step(dve.tensor_scalar(a, a, -PI, None, ALU.max))
            dve.memset(dots[:], 0.0).then_inc(consts_dve, 1)
            dve.wait_ge(consts_dve, 1)
            dve.wait_ge(consts_act, 2)
            dve.sem_inc(dotted, 1)

            def stage(s, prep):
                take_h(s)
                beside(dve, passed["dve"], serve(s), preps(prep) if prep else ())

            for _ in preps(Prep("gla", 0)):
                pass
            with dve.Fori(0, BLOCKS - 1) as s:
                stage(s, Prep("gla", s + 1))
            stage(BLOCKS - 1, Prep("swa", 0))
            with dve.Fori(BLOCKS, STAGES - 1) as s:
                dve.wait_ge(band_made, 1)
                stage(s, Prep("swa", s - (BLOCKS - 1)))
            stage(STAGES - 1, None)

        @block.scalar
        def _(act):
            step = Steps(act, own["act"], passed["act"])

            def say(ins):
                ins.then_inc(said["act"], 1)

            def sqrt(prep, n, var_event):
                said_by(act, "dve", prep, var_event)
                say(act.activation(stat[:, 2, 0:n], stat[:, 1, 0:n], ACT.Sqrt))

            def turned(prep, event, gain=None, at=0):
                said_by(act, "pe", prep, event)
                if gain is None:
                    say(act.activation(actT[:].rearrange("p k t -> p (k t)"), two_banks(0, 1), ACT.Copy))
                    return
                for k in range(KT):
                    src = ps[:, at + k // 4, (k % 4) * P:(k % 4 + 1) * P]
                    scale = 1.0 if gain is None else gain[:, k:k + 1]
                    i = act.activation(actT[:, k, :], src, ACT.Copy, scale=scale)
                    if k < KT - 1:
                        step.mark(i)
                step.settle()
                say(i)

            def normed(prep, at):
                act.wait_ge(x_loaded, (prep.p + prep.layer * BLOCKS) * 16 + 16)
                say(act.activation(junk, xc[:], ACT.Square, accum_out=stat[:, 0, 0:1]))
                yield at["var"]
                sqrt(prep, 1, "var")
                yield at["hT"]
                turned(prep, "hT", gmix[:, prep.layer])

            def gla(prep, at):
                step.restart()
                yield from normed(prep, at)
                yield at["lr"]
                said_by(act, "pe", prep, "lr")
                say(act.activation(lrT[:], ps[0:RANK, 4, 0:P], ACT.Copy))
                yield at["ln"]
                said_by(act, "dve", prep, "absx")
                say(act.activation(g_t, g_t, ACT.Exp, scale=-1.0))
                said_by(act, "act", prep, "exp")
                say(act.activation(g_t, g_t, ACT.Ln, bias=1.0))
                yield at["decay"]
                said_by(act, "dve", prep, "bdiff")
                step.mark(act.activation(g_eb, g_t, ACT.Exp, scale=1.0 / TAU))
                step.mark(act.activation(g_enb, g_t, ACT.Exp, scale=-1.0 / TAU))
                step.settle()
                say(act.activation(g_ef, g_b, ACT.Exp, scale=1.0 / TAU))
                yield at["v"]
                said_by(act, "pe", prep, "v")
                say(act.activation(g_v.rearrange("p h v -> p (h v)"), two_banks(0, 1), ACT.Copy))
                yield at["mask"]
                said_by(act, "pe", prep, "kfT")
                say(act.activation(g_kft, ps[:, 5, :].rearrange("p (h t) -> p h t", h=HEADS_A), ACT.Copy))
                yield at["silu"]
                said_by(act, "pe", prep, "r")
                say(act.activation(g_r.rearrange("p h v -> p (h v)"), two_banks(2, 3), ACT.Silu))
                yield at["state1"]
                said_by(act, "pe", prep, "o")
                for h in range(HEADS_A):
                    i = act.activation(hn.rearrange("p k t -> p (k t)")[:, h * DV:(h + 1) * DV],
                                       two_banks(2, 3)[:, h * DV:(h + 1) * DV], ACT.Square,
                                       accum_out=stat[:, 0, h:h + 1])
                    if h < HEADS_A - 1:
                        step.mark(i)
                step.settle()
                say(i)
                yield at["osqrt"]
                sqrt(prep, HEADS_A, "ovar")
                yield at["oT"]
                turned(prep, "oT", ggla)
                yield from select(prep, at)

            def swa(prep, at):
                step.restart()
                yield from normed(prep, at)
                yield at["qsq"]
                said_by(act, "pe", prep, "q")
                step.mark(act.activation(s_sq[:, 0:HEADS_Q].rearrange("p h d -> p (h d)"), two_banks(0, 1),
                                         ACT.Square))
                said_by(act, "pe", prep, "kv")
                i = act.activation(s_sq[:, HEADS_Q:].rearrange("p h d -> p (h d)"), ps[:, 2, 0:HEADS_KV * HD],
                                   ACT.Square)
                step.settle()
                say(i)
                yield at["qvar"]
                sqrt(prep, HEADS_Q + HEADS_KV, "qvar")
                say(act.activation(kT[:, :, 0:P], kT[:, :, P:2 * P], ACT.Copy))
                yield at["qT"]
                said_by(act, "pe", prep, "qT")
                said_by(act, "act", prep, "kprev")
                step(act.activation(kT[:, :, P:2 * P], ps[:, 2, 0:HEADS_KV * P].rearrange(
                    "p (h t) -> p h t", h=HEADS_KV), ACT.Copy))
                say(act.activation(s_qT.rearrange("p k t -> p (k t)"), two_banks(0, 1), ACT.Copy))
                for g in range(4):
                    yield at[f"g{g}"] + 1
                    said_by(act, "dve", prep, f"m{g}")
                    for j in range(4):
                        i = act.activation(s_p[g % 2][:, j], s_p[g % 2][:, j], ACT.Exp,
                                           bias=mx[:, 0, 4 * g + j:4 * g + j + 1],
                                           accum_out=mx[:, 2, 4 * g + j:4 * g + j + 1])
                        if j < 3:
                            step.mark(i)
                    step.settle()
                    say(i)
                    yield at[f"g{g}"] + 3
                    said_by(act, "pe", prep, f"pT{g}")
                    if g >= 2:
                        said_by(act, "pe", prep, f"o{g - 2}")
                    say(act.activation(s_pT[g % 2].rearrange("p k t -> p (k t)"), two_banks(2, 3), ACT.Copy))
                say(act.activation(mx[:, 1, :], mx[:, 1, :], ACT.Exp))
                yield at["oT"]
                turned(prep, "oT")
                yield from select(prep, at)

            def select(prep, at):
                yield at["x2"]
                said_by(act, "dve", prep, "x2")
                say(act.activation(junk, xc[:], ACT.Square, accum_out=stat[:, 0, 0:1]))
                yield at["var2"]
                sqrt(prep, 1, "var2")
                yield at["h2T"]
                turned(prep, "h2T")
                for b in range(2):
                    yield at["pq" + "ab"[b]]
                    said_by(act, "pe", prep, f"pq{b}")
                    say(act.activation(pqT[:, 4 * b:4 * b + 4, :], ps[:, 2 + b, :].rearrange(
                        "p (h t) -> p h t", h=4), ACT.Copy))
                for part in range(2):
                    yield at["key" + "ab"[part]] - 1
                    hs = slice(part * HEADS_P // 2, (part + 1) * HEADS_P // 2)
                    said_by(act, "dve", prep, f"gshift{part}")
                    say(act.activation(ef[:, 1, hs], ef[:, 0, hs], ACT.Exp))

            def preps(prep):
                return (gla if prep.kind == "gla" else swa)(prep, AT[prep.kind])

            def serve(s):
                def part(r, beat, n):
                    for i in range(beat * BEAT, (beat + n) * BEAT):
                        at = (s * ROUNDS + r) * SLOTS + i
                        act.wait_ge(dotted, at + 2)
                        act.activation(gelu[:, i:i + 1], dots[:, i:i + 1], ACT.Gelu).then_inc(gelued, 1)
                        act.wait_ge(gelued, at + 1)
                        col = (s * ROUNDS + r) * SLOTS + (i - layer[0] * BLOCKS * PICKS)
                        act.activation(coef[:, i:i + 1], gate[:, bass.ds(col, 1)], ACT.Copy,
                                       scale=gelu[:, i:i + 1]).then_inc(weighed, 1)
                        act.wait_ge(weighed, at + 1)
                        if i >= 4:
                            act.wait_ge(used[i - 4], s * ROUNDS + r + 2)
                        else:
                            act.wait_ge(used[i + 4], s * ROUNDS + r + 1)
                        act.activation(diag[:, i % 4, :], ident[:], ACT.Copy,
                                       scale=coef[:, i:i + 1]).then_inc(diag_ready, 1)
                return part

            def close(s):
                act.wait_ge(used[SLOTS - 1], s * ROUNDS + (ROUNDS + 1))
                act.wait_ge(stored, s * 16 + 1)
                for b in range(2):
                    act.activation(y_sb[:, b * 512:(b + 1) * 512], acc[:, b * 512:(b + 1) * 512],
                                   ACT.Copy).then_inc(acc_taken, 1)

            def stage(s, prep):
                beside(act, passed["act"], serve(s), preps(prep) if prep else ())
                close(s)

            act.sem_inc(acc_taken, 1)
            act.sem_inc(stored, 1)
            act.wait_ge(consts_dve, 1)
            for dst, w in ((sinb, 1), (cosb, 2)):
                act.activation(dst[:], angle[:, w].rearrange("p b j -> p (b j)"), ACT.Sin).then_inc(consts_act, 1)
            layer = [0]
            for _ in preps(Prep("gla", 0)):
                pass
            with act.Fori(0, BLOCKS - 1) as s:
                stage(s, Prep("gla", s + 1))
            stage(BLOCKS - 1, Prep("swa", 0))
            layer[0] = 1
            with act.Fori(BLOCKS, STAGES - 1) as s:
                stage(s, Prep("swa", s - (BLOCKS - 1)))
            stage(STAGES - 1, None)

        @block.tensor
        def _(pe):
            def say(ins):
                ins.then_inc(said["pe"], 1)

            def turn(src, at=0):
                for k in range(KT):
                    i = pe.transpose(ps[:, at + k // 4, (k % 4) * P:(k % 4 + 1) * P], src[:, k, :], ident[:])
                say(i)

            def strip(prep, n):
                if n < RESIDENT:
                    if isinstance(prep.p, int):
                        pe.wait_ge(res_loaded[n], 16 * (prep.layer + 1))
                else:
                    pe.wait_ge(slot_loaded[(n - RESIDENT) % 2], prep.slot_uses(n - RESIDENT) * 16)
                return weight(prep, n)

            def left(prep, n, bank, side):
                w = strip(prep, n)
                for c in range(2):
                    for k in range(KT):
                        i = pe.matmul(ps[:, bank, (2 * side + c) * P:(2 * side + c + 1) * P],
                                      w[:, k, c * P:(c + 1) * P], actT[:, k, :], start=(k == 0),
                                      stop=(k == KT - 1))
                return i

            def right(prep, n, dst, bias=None):
                w = strip(prep, n)
                if bias is not None:
                    pe.matmul(dst, ones[0:1, :], bias, start=True, stop=False)
                for k in range(KT):
                    i = pe.matmul(dst, actT[:, k, :], w[:, k, :], start=(k == 0 and bias is None),
                                  stop=(k == KT - 1))
                return i

            def normed(prep, at):
                yield at["hT"]
                said_by(pe, "dve", prep, "h")
                if not (isinstance(prep.p, int) and prep.layer == 0):
                    said_by(pe, "dve", before(prep), "experts1")
                turn(hn)

            def gla(prep, at):
                yield from normed(prep, at)
                yield at["q0"]
                said_by(pe, "act", prep, "hT")
                left(prep, 0, 2, 0)
                yield at["q1"]
                say(left(prep, 1, 2, 1))
                for k in range(KT):
                    i = pe.matmul(ps[0:RANK, 4, 0:P], wlr[:, k, :], actT[:, k, :], start=(k == 0), stop=(k == KT - 1))
                say(i)
                yield at["k0"]
                left(prep, 2, 3, 0)
                yield at["k1"]
                say(left(prep, 3, 3, 1))
                said_by(pe, "act", prep, "lr")
                pe.wait_ge(small_loaded, (prep.p + prep.layer * BLOCKS) * 16 + 16)
                for h in range(HEADS_A):
                    i = pe.matmul(ps[:, 5, h * P:(h + 1) * P], walpha[:, h * DK:(h + 1) * DK], lrT[:], start=True,
                                  stop=True)
                say(i)
                for n in range(4):
                    yield at[f"v{n}"]
                    i = right(prep, 4 + n, two_banks(0, 1)[:, n * STRIP:(n + 1) * STRIP])
                    if 4 + n >= RESIDENT and n < 3:
                        used_up(i)
                say(i)
                yield at["attn"]
                said_by(pe, "dve", prep, "qd")
                for h in range(HEADS_A):
                    i = pe.matmul(ps[:, 4, h * P:(h + 1) * P], g_kinv[:, h], g_qd[:, h], start=True, stop=True)
                say(i)
                said_by(pe, "dve", prep, "kf")
                for h in range(HEADS_A):
                    i = pe.transpose(ps[:, 5, h * P:(h + 1) * P], g_kf[:, h], ident[:])
                say(i)
                for n in range(4):
                    yield at[f"r{n}"]
                    i = right(prep, 8 + n, two_banks(2, 3)[:, n * STRIP:(n + 1) * STRIP])
                    if n < 3:
                        used_up(i)
                say(i)
                yield at["upd"]
                said_by(pe, "act", prep, "kf")
                said_by(pe, "dve", prep, "attn")
                for c in range(2):
                    rows = slice(c * CHUNK, (c + 1) * CHUNK)
                    for h in range(HEADS_A):
                        i = pe.matmul(two_banks(4 * c, 4 * c + 1)[:, h * DV:(h + 1) * DV], g_kft[rows, h, :],
                                      g_v[rows, h, :], start=True, stop=True)
                say(i)
                for h in range(HEADS_A):
                    if h % 2 == 0:
                        yield at[f"o{h // 2}"]
                        said_by(pe, "act", prep, "silu")
                        said_by(pe, "dve", prep, "state0")
                    o = two_banks(2, 3)[:, h * DV:(h + 1) * DV]
                    pe.matmul(o, attnT[:, h], g_v[:, h], start=True, stop=True)
                    pe.matmul(o[0:CHUNK], g_qd[:, h, 0:CHUNK], state0[:, h], start=False, stop=True,
                              skip_group_check=True)
                    i = pe.matmul(o[CHUNK:P], g_qd[:, h, CHUNK:P], state1[:, h], start=False, stop=True,
                                  skip_group_check=True)
                say(i)
                yield at["oT"]
                said_by(pe, "dve", prep, "o")
                turn(g_o.rearrange("p h (a t) -> p (h a) t", t=P))
                yield from select(prep, at)

            def swa(prep, at):
                yield from normed(prep, at)
                for n in range(4):
                    yield at[f"q{n}"]
                    if n == 0:
                        said_by(pe, "act", prep, "hT")
                        pe.wait_ge(small_loaded, (prep.p + prep.layer * BLOCKS) * 16 + 16)
                    i = right(prep, n, two_banks(0, 1)[:, n * STRIP:(n + 1) * STRIP],
                              bias_in[:, n * STRIP:(n + 1) * STRIP])
                say(i)
                yield at["kv"]
                say(right(prep, 4, ps[:, 2, 0:STRIP], bias_in[:, 4 * STRIP:5 * STRIP]))
                yield at["qT"]
                said_by(pe, "dve", prep, "qk")
                for h in range(HEADS_KV):
                    pe.transpose(ps[:, 2, h * P:(h + 1) * P], s_kdup[:, h].rearrange("p a d -> p (a d)"), ident[:])
                turn(s_qk[:, 0:HEADS_Q].rearrange("p (k a) d -> p k (a d)", a=2))
                for g in range(4):
                    yield at[f"g{g}"]
                    said_by(pe, "act", prep, "qT")
                    if g >= 1:
                        said_by(pe, "dve", prep, f"m{g - 1}")
                    for j in range(2):
                        for par in range(2):
                            i = pe.matmul(ps[:, par, j * 2 * P:(j + 1) * 2 * P],
                                          s_qT[par * HD:(par + 1) * HD, 2 * g + j, :],
                                          kT[par * HD:(par + 1) * HD, g // 2, :], start=True, stop=True)
                    say(i)
                    yield at[f"g{g}"] + 2
                    said_by(pe, "act", prep, f"p{g}")
                    if g >= 1:
                        said_by(pe, "act", prep, f"pT{g - 1}")
                    for j in range(4):
                        for b in range(2):
                            m = 2 * j + b
                            i = pe.transpose(ps[:, 2 + m // 4, (m % 4) * P:(m % 4 + 1) * P],
                                             s_p[g % 2][:, j, b * P:(b + 1) * P], ident[:])
                    say(i)
                    yield at[f"g{g}"] + 4
                    said_by(pe, "act", prep, f"pT{g}")
                    for par in range(2):
                        for j in range(2):
                            h = 4 * g + 2 * j + par
                            for b in range(2):
                                i = pe.matmul(two_banks(4, 5)[:, h * HD:(h + 1) * HD],
                                              s_pT[g % 2][:, 2 * (2 * par + j) + b, :],
                                              vv[:, b, (g // 2) * HD:(g // 2 + 1) * HD],
                                              start=(b == 0), stop=(b == 1))
                    say(i)
                yield at["oT"]
                said_by(pe, "dve", prep, "o")
                turn(s_o.rearrange("p (k a) d -> p k (a d)", a=2))
                yield from select(prep, at)

            def used_up(ins):
                ins.then_inc(strip_used, 1)

            def select(prep, at):
                n0 = out0(prep)
                for n in range(4):
                    yield at[f"out{n}"]
                    said_by(pe, "act", prep, "oT")
                    bias = bias_out[:, n * STRIP:(n + 1) * STRIP] if prep.layer else None
                    if prep.layer and n == 0:
                        pe.wait_ge(bias_loaded, prep.p * 16 + 16)
                    i = right(prep, n0 + n, two_banks(4, 5)[:, n * STRIP:(n + 1) * STRIP], bias)
                    if n0 + n >= RESIDENT and n < 3:
                        used_up(i)
                say(i)
                yield at["h2T"]
                said_by(pe, "dve", prep, "h2")
                turn(h_next[:].rearrange("p (k t) -> p k t", k=KT))
                yield at["pq0"]
                said_by(pe, "act", prep, "h2T")
                pe.wait_ge(keys_loaded, 16 * (prep.layer + 1))
                for b in range(2):
                    yield at[f"pq{2 * b}"]
                    used_up(left(prep, pq0(prep) + 2 * b, 2 + b, 0))
                    yield at[f"pq{2 * b + 1}"]
                    say(left(prep, pq0(prep) + 2 * b + 1, 2 + b, 1))
                    yield at["sc" + "ab"[b]]
                    said_by(pe, "act", prep, f"pq{b}")
                    for h in range(4 * b, 4 * b + 4):
                        for half in range(2):
                            rows = slice(half * HALF, (half + 1) * HALF)
                            i = pe.matmul(ps[:, 4 * half + b, (h % 4) * KEYS:(h % 4 + 1) * KEYS],
                                          pqT[rows, h, :], keysT[rows, h, :], start=True, stop=True)
                    say(i)

            def preps(prep):
                return (gla if prep.kind == "gla" else swa)(prep, AT[prep.kind])

            def serve(s):
                def part(r, beat, n):
                    for i in range(beat * BEAT, (beat + n) * BEAT):
                        pe.wait_ge(diag_ready, (s * ROUNDS + r) * SLOTS + (i + 1))
                        for b in range(2):
                            m = pe.matmul(acc[:, b * 512:(b + 1) * 512], diag[:, i % 4, :],
                                          ring[:, i, D + b * 512:D + (b + 1) * 512], start=False, stop=True,
                                          skip_group_check=True)
                        m.then_inc(used[i], 1)
                return part

            def seed(s, prep):
                pe.wait_ge(acc_taken, s * 2 + 1)
                said_by(pe, "dve", prep, "x2")
                for b in range(2):
                    m = pe.matmul(acc[:, b * 512:(b + 1) * 512], ident[:], xc[:, b * 512:(b + 1) * 512],
                                  start=True, stop=True)
                m.then_inc(seeded, 1)

            def stage(s, mine, prep):
                seed(s, mine)
                beside(pe, passed["pe"], serve(s), preps(prep) if prep else ())

            pe.wait_ge(consts_made, N_CONST_MADE)
            pe.wait_ge(consts_loaded, 16 * N_CONST_LOADS)
            for _ in preps(Prep("gla", 0)):
                pass
            with pe.Fori(0, BLOCKS - 1) as s:
                stage(s, Prep("gla", s), Prep("gla", s + 1))
            stage(BLOCKS - 1, Prep("gla", BLOCKS - 1), Prep("swa", 0))
            with pe.Fori(BLOCKS, STAGES - 1) as s:
                stage(s, Prep("swa", s - BLOCKS), Prep("swa", s - (BLOCKS - 1)))
            stage(STAGES - 1, Prep("swa", BLOCKS - 1), None)


def in_strips(w):
    n = w.shape[1] // STRIP
    return w.reshape(KT, P, n, STRIP).transpose(2, 1, 0, 3).reshape(n, P, KT * STRIP)


def kernel(x, positions, ln_mix, ln_ffn, gla_w_in, gla_w_alpha, gla_b_alpha, gla_norm, gla_w_out, swa_w_in, swa_b_in,
           swa_q_norm, swa_k_norm, swa_sinks, swa_w_out, swa_b_out, peer_w_q, peer_keys, peer_u, peer_v):
    from concourse import bacc
    from concourse.bass_utils import run_bass_kernel_spmd

    a = {k: np.asarray(v) for k, v in dict(
        x=x, positions=positions, ln_mix=ln_mix, ln_ffn=ln_ffn, w_in=gla_w_in, w_alpha=gla_w_alpha,
        b_alpha=gla_b_alpha, norm=gla_norm, w_out=gla_w_out, sw_in=swa_w_in, sb_in=swa_b_in, qn=swa_q_norm,
        kn=swa_k_norm, sinks=swa_sinks, sw_out=swa_w_out, sb_out=swa_b_out, wq=peer_w_q, keys=peer_keys,
        u=peer_u, v=peer_v).items()}
    wide = HEADS_A * (2 * DK + 2 * DV)
    keys = a["keys"].transpose(0, 2, 4, 1, 3).reshape(2, P, HEADS_P, KEYS)
    arrays = {
        "in_x": a["x"][0],
        "in_positions": a["positions"][0].reshape(BLOCKS, P).T,
        "in_gain_mix": a["ln_mix"].reshape(2, KT, P).transpose(2, 0, 1),
        "in_gain_ffn": a["ln_ffn"],
        "in_strips0": np.concatenate([in_strips(w) for w in (a["w_in"][0][:, :wide], a["w_out"][0], a["wq"][0])]),
        "in_strips1": np.concatenate([in_strips(w) for w in (a["sw_in"][0], a["sw_out"][0], a["wq"][1])]),
        "in_w_lr": a["w_in"][0][:, wide:].reshape(KT, P, RANK).transpose(1, 0, 2),
        "in_w_alpha": a["w_alpha"][0],
        "in_b_alpha": a["b_alpha"][0].reshape(HEADS_A, DK).T,
        "in_gla_gain": a["norm"][0].reshape(KT, P).T,
        "in_b_in": a["sb_in"],
        "in_b_out": a["sb_out"],
        "in_qk_gain": np.concatenate([a["qn"], a["kn"]], axis=1),
        "in_sinks": a["sinks"],
        "in_keys0": keys[0],
        "in_keys1": keys[1],
        "in_uv0": np.concatenate([a["u"][0], a["v"][0]], axis=1),
        "in_uv1": np.concatenate([a["u"][1], a["v"][1]], axis=1),
    }
    arrays = {k: np.ascontiguousarray(v) for k, v in arrays.items()}
    nc = bacc.Bacc("TRN2", target_bir_lowering=False, num_devices=1)
    args = [nc.dram_tensor(k, v.shape, mybir.dt.from_np(v.dtype), kind="ExternalInput").ap()
            for k, v in arrays.items()]
    out = nc.dram_tensor("out_0", [SEQ, D], F32, kind="ExternalOutput").ap()
    build(nc, *args, out)
    r = run_bass_kernel_spmd(nc, [arrays], core_ids=[0])
    return r.results[0]["out_0"].reshape(1, SEQ, D)
```
